# Optimizing a Trainium2 kernel written in Bass

```python
import jax, jax.numpy as jnp
from jax import lax
import numpy as np

D_MODEL = 1024
BATCH = 1
SEQ = 512
DEPTH = 2
DEC_BATCH = 8
DEC_SEQ = 16
PAST_LEN = 512

CHUNK = 64
D_FF = 2816
N_HEADS = 8
N_KV_HEADS = 2
HEAD_DIM = 64
GROUP = N_HEADS // N_KV_HEADS
WINDOW = 128
WIN_CHUNKS = WINDOW // CHUNK
ATT_SCALE = HEAD_DIM ** -0.5
ATT_WIDTH = N_HEADS * HEAD_DIM
KV_WIDTH = N_KV_HEADS * HEAD_DIM
POOL_WIDTH = 256
POOL_WINDOWS = (2, 4, 8, 16)
N_POOL_GROUPS = 4
POOL_GROUP = POOL_WIDTH // N_POOL_GROUPS
POOL_HIST = 15
CONV_WIDTH = 256
CONV_K = 3
CONV_HIST = CONV_K - 1
N_BRANCH = 3
MIX_WIDTH = POOL_WIDTH + ATT_WIDTH + CONV_WIDTH
IN_WIDTH = POOL_WIDTH + ATT_WIDTH + 2 * KV_WIDTH + 3 * CONV_WIDTH + N_BRANCH * D_MODEL
N_NORMS = 6
RMS_EPS = 1e-6

kernel_name = "hybrid_streaming_pool_swa_conv_step"

def _rmsnorm(x, g):
    xf = x.astype(jnp.float32)
    y = xf * lax.rsqrt(jnp.mean(xf * xf, axis=-1, keepdims=True) + RMS_EPS)
    return (y * g.astype(jnp.float32)).astype(x.dtype)

def _swiglu(x, w_gate, w_up, w_down):
    return (jax.nn.silu(x @ w_gate) * (x @ w_up)) @ w_down

def _pool_mixer(p, hist, pos0, w_pool, pool_scale):
    bsz, n = p.shape[0], p.shape[1]
    ext = jnp.concatenate([hist, p], axis=1)
    cs = jnp.pad(jnp.cumsum(ext.astype(jnp.float32), axis=1), ((0, 0), (1, 0), (0, 0)))
    end = cs[:, POOL_HIST + 1:]
    pos = (pos0 + jnp.arange(n))[None, :, None]
    means = []
    for gi, w in enumerate(POOL_WINDOWS):
        lo, hi = gi * POOL_GROUP, (gi + 1) * POOL_GROUP
        start = cs[:, POOL_HIST + 1 - w: POOL_HIST + 1 - w + n, lo:hi]
        cnt = jnp.minimum(pos + 1, w).astype(jnp.float32)
        means.append((end[:, :, lo:hi] - start) / cnt)
    d = (jnp.concatenate(means, axis=-1) - p.astype(jnp.float32)).astype(p.dtype)
    d = d.reshape(bsz, n, N_POOL_GROUPS, POOL_GROUP)
    y = jnp.einsum("bsgc,gcd->bsgd", d, w_pool).reshape(bsz, n, POOL_WIDTH)
    return y * pool_scale, ext[:, -POOL_HIST:]

def _conv_mixer(bgate, cgate, x_in, hist, w_conv):
    n = x_in.shape[1]
    ext = jnp.concatenate([hist, cgate * x_in], axis=1)
    z = sum(ext[:, j:j + n] * w_conv[j] for j in range(CONV_K))
    return bgate * z, ext[:, -CONV_HIST:]

def _sink_softmax(s, sink):
    sink = sink.astype(jnp.float32)
    m = jnp.maximum(jnp.max(s, axis=-1, keepdims=True), sink)
    e = jnp.exp(s - m)
    return e / (jnp.sum(e, axis=-1, keepdims=True) + jnp.exp(sink - m))

def _attn_prompt(q, k, v, sinks):
    bsz, n = q.shape[0], q.shape[1]
    nc = n // CHUNK
    span = WIN_CHUNKS * CHUNK
    qb = q.reshape(bsz, nc, CHUNK, N_KV_HEADS, GROUP, HEAD_DIM)

    def band(t):
        tb = t.reshape(bsz, nc, CHUNK, N_KV_HEADS, HEAD_DIM)
        tb = jnp.pad(tb, ((0, 0), (WIN_CHUNKS - 1, 0), (0, 0), (0, 0), (0, 0)))
        return jnp.concatenate([tb[:, j:j + nc] for j in range(WIN_CHUNKS)], axis=2)

    kb, vb = band(k), band(v)
    s = jnp.einsum("bcqkgd,bcjkd->bckgqj", qb, kb, preferred_element_type=jnp.float32) * ATT_SCALE
    key_chunk = jnp.arange(nc)[:, None] - (WIN_CHUNKS - 1) + jnp.arange(span)[None, :] // CHUNK
    s = jnp.where((key_chunk >= 0)[None, :, None, None, None, :], s, -jnp.inf)
    pr = _sink_softmax(s, sinks.reshape(N_KV_HEADS, GROUP, 1, 1))
    o = jnp.einsum("bckgqj,bcjkd->bcqkgd", pr.astype(v.dtype), vb)
    return o.reshape(bsz, n, ATT_WIDTH)

def _attn_sample(q, k, v, ck, cv, sinks):
    bsz, n = q.shape[0], q.shape[1]
    r = ck.shape[1]
    kk = jnp.concatenate([ck, k], axis=1)
    vv = jnp.concatenate([cv, v], axis=1)
    qpos = PAST_LEN + jnp.arange(n)
    kpos = PAST_LEN - r + jnp.arange(r + n)
    qc, kc = qpos // CHUNK, kpos // CHUNK
    allowed = (kpos >= 0)[None, :] & (kc[None, :] <= qc[:, None]) & (kc[None, :] >= qc[:, None] - (WIN_CHUNKS - 1))
    qg = q.reshape(bsz, n, N_KV_HEADS, GROUP, HEAD_DIM)
    s = jnp.einsum("bqkgd,bjkd->bkgqj", qg, kk, preferred_element_type=jnp.float32) * ATT_SCALE
    s = jnp.where(allowed[None, None, None], s, -jnp.inf)
    pr = _sink_softmax(s, sinks.reshape(N_KV_HEADS, GROUP, 1, 1))
    o = jnp.einsum("bkgqj,bjkd->bqkgd", pr.astype(vv.dtype), vv)
    return o.reshape(bsz, n, ATT_WIDTH), kk[:, -r:], vv[:, -r:]

def _mixer(u, pos0, pool_hist, conv_hist, ck, cv, w_in, b_gate, w_pool, pool_scale, sinks, w_conv, w_branch, w_out):
    bsz, n, _ = u.shape
    proj = u @ w_in
    cuts = [POOL_WIDTH, ATT_WIDTH, KV_WIDTH, KV_WIDTH, CONV_WIDTH, CONV_WIDTH, CONV_WIDTH]
    idx = [int(i) for i in np.cumsum(cuts)]
    p, q, k, v, bg, cg, xc, gl = jnp.split(proj, idx, axis=-1)
    y_pool, new_pool = _pool_mixer(p, pool_hist, pos0, w_pool, pool_scale)
    q = q.reshape(bsz, n, N_HEADS, HEAD_DIM)
    k = k.reshape(bsz, n, N_KV_HEADS, HEAD_DIM)
    v = v.reshape(bsz, n, N_KV_HEADS, HEAD_DIM)
    if ck is None:
        y_att = _attn_prompt(q, k, v, sinks)
        rows = min(WINDOW, n)
        new_k, new_v = k[:, -rows:], v[:, -rows:]
    else:
        y_att, new_k, new_v = _attn_sample(q, k, v, ck, cv, sinks)
    y_conv, new_conv = _conv_mixer(bg, cg, xc, conv_hist, w_conv)
    gates = jax.nn.sigmoid(gl.reshape(bsz, n, N_BRANCH, D_MODEL) + b_gate.reshape(N_BRANCH, D_MODEL))
    a0, a1 = POOL_WIDTH, POOL_WIDTH + ATT_WIDTH
    merged = (gates[:, :, 0] * (y_pool @ w_branch[:a0])
              + gates[:, :, 1] * (y_att @ w_branch[a0:a1])
              + gates[:, :, 2] * (y_conv @ w_branch[a1:]))
    return merged @ w_out, new_pool, new_conv, new_k, new_v

def _layer(h, pos0, pool_hist, conv_hist, ck, cv, g, f1g, f1u, f1d, w_in, b_gate, w_pool, pool_scale,
           sinks, w_conv, w_branch, w_out, f2g, f2u, f2d):
    h = h + 0.5 * _rmsnorm(_swiglu(_rmsnorm(h, g[0]), f1g, f1u, f1d), g[1])
    m, new_pool, new_conv, new_k, new_v = _mixer(_rmsnorm(h, g[2]), pos0, pool_hist, conv_hist, ck, cv,
                                               w_in, b_gate, w_pool, pool_scale, sinks, w_conv, w_branch, w_out)
    h = h + _rmsnorm(m, g[3])
    h = h + 0.5 * _rmsnorm(_swiglu(_rmsnorm(h, g[4]), f2g, f2u, f2d), g[5])
    return h, new_pool, new_conv, new_k, new_v

def setup_inputs(seed: int = 0) -> dict:
    key = jax.random.key(seed)
    ks = jax.random.split(key, 24)
    f32 = jnp.float32

    def nrm(k, shape, scale):
        return jax.random.normal(k, shape, f32) * scale

    kv_rows = min(WINDOW, PAST_LEN)
    return {
        "x_prompt": nrm(ks[0], (BATCH, SEQ, D_MODEL), 1.0),
        "x_sample": nrm(ks[1], (DEC_BATCH, DEC_SEQ, D_MODEL), 1.0),
        "state_pool": nrm(ks[2], (DEPTH, DEC_BATCH, POOL_HIST, POOL_WIDTH), 1.0),
        "state_conv": nrm(ks[3], (DEPTH, DEC_BATCH, CONV_HIST, CONV_WIDTH), 1.0),
        "cache_k": nrm(ks[4], (DEPTH, DEC_BATCH, kv_rows, N_KV_HEADS, HEAD_DIM), 1.0),
        "cache_v": nrm(ks[5], (DEPTH, DEC_BATCH, kv_rows, N_KV_HEADS, HEAD_DIM), 1.0),
        "norm_g": 1.0 + nrm(ks[6], (DEPTH, N_NORMS, D_MODEL), 0.02),
        "ffn1_w_gate": nrm(ks[7], (DEPTH, D_MODEL, D_FF), D_MODEL ** -0.5),
        "ffn1_w_up": nrm(ks[8], (DEPTH, D_MODEL, D_FF), D_MODEL ** -0.5),
        "ffn1_w_down": nrm(ks[9], (DEPTH, D_FF, D_MODEL), D_FF ** -0.5),
        "w_in": nrm(ks[10], (DEPTH, D_MODEL, IN_WIDTH), D_MODEL ** -0.5),
        "b_gate": nrm(ks[11], (DEPTH, N_BRANCH * D_MODEL), 0.02),
        "w_pool": nrm(ks[12], (DEPTH, N_POOL_GROUPS, POOL_GROUP, POOL_GROUP), POOL_GROUP ** -0.5),
        "pool_scale": 1.0 + nrm(ks[13], (DEPTH, POOL_WIDTH), 0.02),
        "sinks": nrm(ks[14], (DEPTH, N_HEADS), 0.5),
        "w_conv": nrm(ks[15], (DEPTH, CONV_K, CONV_WIDTH), CONV_K ** -0.5),
        "w_branch": nrm(ks[16], (DEPTH, MIX_WIDTH, D_MODEL), POOL_WIDTH ** -0.5),
        "w_out": nrm(ks[17], (DEPTH, D_MODEL, D_MODEL), D_MODEL ** -0.5),
        "ffn2_w_gate": nrm(ks[18], (DEPTH, D_MODEL, D_FF), D_MODEL ** -0.5),
        "ffn2_w_up": nrm(ks[19], (DEPTH, D_MODEL, D_FF), D_MODEL ** -0.5),
        "ffn2_w_down": nrm(ks[20], (DEPTH, D_FF, D_MODEL), D_FF ** -0.5),
    }

def reference(x_prompt, x_sample, state_pool, state_conv, cache_k, cache_v, norm_g, ffn1_w_gate, ffn1_w_up,
              ffn1_w_down, w_in, b_gate, w_pool, pool_scale, sinks, w_conv, w_branch, w_out,
              ffn2_w_gate, ffn2_w_up, ffn2_w_down):
    bp = x_prompt.shape[0]
    hp, hs = x_prompt, x_sample
    pool_p, conv_p, k_p, v_p = [], [], [], []
    pool_s, conv_s, k_s, v_s = [], [], [], []
    for l in range(DEPTH):
        lw = (norm_g[l], ffn1_w_gate[l], ffn1_w_up[l], ffn1_w_down[l], w_in[l], b_gate[l], w_pool[l],
              pool_scale[l], sinks[l], w_conv[l], w_branch[l], w_out[l], ffn2_w_gate[l], ffn2_w_up[l],
              ffn2_w_down[l])
        zero_pool = jnp.zeros((bp, POOL_HIST, POOL_WIDTH), x_prompt.dtype)
        zero_conv = jnp.zeros((bp, CONV_HIST, CONV_WIDTH), x_prompt.dtype)
        hp, a, b, c, d = _layer(hp, 0, zero_pool, zero_conv, None, None, *lw)
        pool_p.append(a); conv_p.append(b); k_p.append(c); v_p.append(d)
        hs, a, b, c, d = _layer(hs, PAST_LEN, state_pool[l], state_conv[l], cache_k[l], cache_v[l], *lw)
        pool_s.append(a); conv_s.append(b); k_s.append(c); v_s.append(d)
    return (hp, hs,
            jnp.stack(pool_p), jnp.stack(conv_p), jnp.stack(k_p), jnp.stack(v_p),
            jnp.stack(pool_s), jnp.stack(conv_s), jnp.stack(k_s), jnp.stack(v_s))


_drawn_inputs = setup_inputs


def setup_inputs(seed=0):
    import zlib

    import numpy as np

    out = dict(_drawn_inputs(seed))
    spreads = {}
    factors = {'b_gate': 6.921, 'pool_scale': 4.25, 'sinks': 8.0}
    for name, (base, spread) in spreads.items():
        noise = np.random.default_rng([zlib.crc32(name.encode()), seed]).standard_normal(out[name].shape)
        drawn = base * np.exp(spread * noise) if base else spread * noise
        out[name] = __import__('jax').numpy.asarray(drawn.astype(out[name].dtype))
    for name, factor in factors.items():
        out[name] = (out[name] * factor).astype(out[name].dtype)
    return out
```

```python
from contextlib import ExitStack

import numpy as np

import concourse.bass as bass
import concourse.mybir as mybir

F32 = mybir.dt.float32
F32R = mybir.dt.float32r
ALU = mybir.AluOpType
ACT = mybir.ActivationFunctionType
AX = mybir.AxisListType.X
ds = bass.ds

P = 128
D = 1024
SEQ, DEC_B, DEC_T = 512, 8, 16
DEPTH = 2
NT = SEQ + DEC_B * DEC_T
HT = NT // 2
HP = SEQ - HT
KD = D // P
FF = 2816
NF = FF // P
FG = NF // 2
CHUNK, HD, NH, NKV = 64, 64, 8, 2
NG = NH // NKV
WIN = 128
PH, CH_ = 15, 2
PW = CW = 256
EPS = 1e-6
SCALE = HD ** -0.5
COL_P, COL_Q, COL_K, COL_V, COL_BG, COL_CG, COL_XC, COL_GATE = 0, 256, 768, 896, 1024, 1280, 1536, 1792
IN_W = COL_GATE + 3 * D
KEYS_S = CHUNK + DEC_T

FFN_PAIRS = 2 * (FG + KD // 2)
MIX_PROJ = 7
MIX_PAIRS = MIX_PROJ + 2 * KD + KD // 2
PAIRS = 2 * FFN_PAIRS + MIX_PAIRS
MIX_GROUPS = 4 * MIX_PROJ + 12 * KD + 2 * KD
GROUPS = 8 * FFN_PAIRS + MIX_GROUPS
FFN_PAIR0 = (0, FFN_PAIRS + MIX_PAIRS)
FFN_GROUP0 = (0, 4 * FFN_PAIRS + MIX_GROUPS)
MIX_PAIR0, MIX_GROUP0 = FFN_PAIRS, 4 * FFN_PAIRS
LOADS = 4

PC_G, PC_BG, PC_PS, PC_WC = 0, 48, 72, 74
NPC = 80

PE_W, CE_W = PH + SEQ + DEC_B * (PH + DEC_T), CH_ + SEQ + DEC_B * (CH_ + DEC_T)
ATT_STEPS = SEQ // CHUNK + 2
STATS = 4
KV_STORES = 2 + 2 * DEC_B
STORES = 4 + 2 * DEC_B
CONST_DMAS = 3 + DEPTH * 4 + 2 + DEC_B + 2
DVE_STEPS = 3 * 16 + 4 * ATT_STEPS + 4 + 2 * KD
POOL_STEPS = 3 * 4 + 3 + 8 + 2 + 6
SQUARES = 32

SEAM_SQ = [("y", 0), ("y", 1), ("y", 2), ("x", 0), ("x", 1), ("x", 2), ("y", 3)] + [("x", j) for j in range(3, 16)]


def trunk_kernel(nc, x_prompt, x_sample, state_pool, state_conv, cache_k, cache_v, norm_g, ffn1_w_gate,
                 ffn1_w_up, ffn1_w_down, w_in, b_gate, w_pool, pool_scale, sinks, w_conv, w_branch, w_out,
                 ffn2_w_gate, ffn2_w_up, ffn2_w_down, c_ident, c_ones, c_count,
                 o_yp, o_ys, o_poolp, o_convp, o_kp, o_vp, o_pools, o_convs, o_ks, o_vs):
    w_ffn = ((ffn1_w_gate, ffn1_w_up, ffn1_w_down), (ffn2_w_gate, ffn2_w_up, ffn2_w_down))
    ctx = ExitStack()
    with ctx:
        base = (nc.sbuf_base + 63) // 64 * 64
        cursor = [base]

        def take(nbytes):
            at = cursor[0]
            cursor[0] += (nbytes + 31) // 32 * 32
            return at

        def view(name, cols, at, dt=F32):
            return nc.alloc_sbuf_tensor_at(name, [P, cols], dt, offset=at)

        def own(name, cols, dt=F32):
            return view(name, cols, take(4 * cols), dt)

        TB = 4 * NT
        at_h, at_x, at_mid, at_y = take(KD * TB), take(2 * KD * TB), take(24 * TB), take(KD * TB)
        h = view("h", KD * NT, at_h)
        x_hi = view("x_hi", KD * NT, at_x, F32R)
        x_lo = view("x_lo", KD * NT, at_x + KD * TB, F32R)
        y_mix = view("y_mix", KD * NT, at_x)
        mid_hi = view("mid_hi", FG * NT, at_mid, F32R)
        mid_lo = view("mid_lo", FG * NT, at_mid + FG * TB, F32R)
        br_hi = view("br_hi", KD * NT, at_mid, F32R)
        br_lo = view("br_lo", KD * NT, at_mid + KD * TB, F32R)
        mg_lo = view("mg_lo", KD * NT, at_mid + 2 * KD * TB, F32R)
        rows = view("rows", 5 * D, at_mid)
        in_mid = [at_mid + 2 * KD * TB]

        def in_mg(name, cols):
            at = in_mid[0]
            in_mid[0] += (4 * cols + 31) // 32 * 32
            return view(name, cols, at)

        p_ext = in_mg("p_ext", 2 * PE_W)
        c_ext = in_mg("c_ext", 2 * CE_W)
        win_a, win_b = in_mg("win_a", PE_W), in_mg("win_b", PE_W)
        assert in_mid[0] <= at_mid + 3 * KD * TB
        y_ffn = view("y_ffn", KD * NT, at_y)
        mg_hi = view("mg_hi", KD * NT, at_y, F32R)
        q_t = view("q_t", 4 * NT, at_y)
        k_t = view("k_t", NT, at_y + 4 * TB)
        v_t = view("v_t", NT, at_y + 5 * TB)
        d_pool = view("d_pool", 2 * NT, at_y + 6 * TB)

        raw = [own(f"raw{s}", FG * P) for s in range(2)]
        w_hi = [own(f"w_hi{s}", FG * P, F32R) for s in range(2)]
        w_lo = [own(f"w_lo{s}", FG * P, F32R) for s in range(2)]

        at_tmp = take(8 * 4 * HT + 256)
        scaled = [view(f"scaled{s}", HT, at_tmp + 4 * HT * s) for s in range(2)]
        silu = [view(f"silu{s}", HT, at_tmp + 4 * HT * (2 + s)) for s in range(2)]
        up = [view(f"up{s}", HT, at_tmp + 4 * HT * (4 + s)) for s in range(2)]
        mid = [view(f"mid{s}", HT, at_tmp + 4 * HT * (6 + s)) for s in range(2)]
        sig = [view(f"sig{s}", HT, at_tmp + 4 * HT * (2 + s)) for s in range(6)]
        PB = 4 * (WIN + 1) + 4
        prob = [view(f"prob{s}", PB, at_tmp + 4 * PB * s) for s in range(3)]
        prob_t = [view(f"prob_t{s}", 4 * P, at_tmp + 12 * PB + 16 * P * s) for s in range(2)]
        assert 12 * PB + 32 * P <= 8 * 4 * HT + 256

        at_seam = take(12 * 4 * HT)
        sq, root, inv_y, acc_y, acc_x, tb = (
            [view(f"{n}{s}", HT, at_seam + 4 * HT * (2 * i + s)) for s in range(2)]
            for i, n in enumerate(("sq", "root", "inv_y", "acc_y", "acc_x", "tb")))
        tb.append(own("tb2", HT))
        v_win = view("v_win", 8 * P, at_seam)
        win_v = view("win_v", PE_W, at_seam + 32 * P)
        assert 32 * P + 4 * PE_W <= 6 * 4 * HT
        inv_x = [own(f"inv_x{s}", HT) for s in range(2)]
        xv = [own(f"xv{s}", HT) for s in range(2)]
        k_s = own("k_s", DEC_B * KEYS_S)
        at_vs = take(4 * DEC_B * P)
        v_s = view("v_s", DEC_B * P, at_vs)
        pc_out = view("pc_out", 8 * P, at_vs)
        at_kr = take(16 * P)
        k_raw = view("k_raw", 4 * P, at_kr)
        prm_rows = view("prm_rows", DEPTH * P, at_kr)
        at_sr = take(4 * (PW + CW))
        sp_raw, sc_raw = view("sp_raw", PW, at_sr), view("sc_raw", CW, at_sr + 4 * PW)
        new_rows = view("new_rows", 4 * P, at_sr)
        kv_out = own("kv_out", 3 * P)
        wp = own("wp", DEPTH * 2 * P)
        wp_now = own("wp_now", 2 * P)
        ident, ones = own("ident", P), own("ones", P)
        count = own("count", 2 * 17)
        prm = own("prm", DEPTH * NPC)
        sink_p, sink_s = own("sink_p", DEPTH * 4), own("sink_s", DEPTH)
        sink_s4 = own("sink_s4", DEPTH * 4)
        row_max, neg, den, rden = own("row_max", 4), own("neg", 4), own("den", 4), own("rden", 4)
        wc_now = own("wc_now", 6)
        eps1, eps4 = own("eps1", 1), own("eps4", 1)
        assert cursor[0] <= nc.sbuf_usable_end, (cursor[0], nc.sbuf_usable_end)
        ctx.enter_context(nc.sbuf_tensor("arena", [P, (cursor[0] - nc.sbuf_base) // 4 - 1], F32))
        ps = ctx.enter_context(nc.psum_tensor("ps", [P, 8, 512], F32))
        BY, BX = (4, 5), (6, 7)

        def sem(name):
            return ctx.enter_context(nc.semaphore(name))

        raw_loaded = [sem("raw_loaded0"), sem("raw_loaded1")]
        w_hi_made = sem("w_hi_made")
        w_split = sem("w_split")
        group_done = sem("group_done")
        evac = sem("evac")
        silu_done = sem("silu_done")
        mid_made = sem("mid_made")
        mid_hi_made = sem("mid_hi_made")
        mid_split = sem("mid_split")
        sq_made = sem("sq_made")
        sq_added = sem("sq_added")
        stat_done = sem("stat_done")
        root_made = sem("root_made")
        inv_made = sem("inv_made")
        h_ready = sem("h_ready")
        x_hi_made = sem("x_hi_made")
        x_ready = sem("x_ready")
        sig_done = sem("sig_done")
        merged = sem("merged")
        mg_hi_made = sem("mg_hi_made")
        mg_ready = sem("mg_ready")
        dve_step, act_step, pool_step = sem("dve_step"), sem("act_step"), sem("pool_step")
        turned = sem("turned")
        turned_out = sem("turned_out")
        scores_half = sem("scores_half")
        scores_done, exp_in, exp_done = sem("scores_done"), sem("exp_in"), sem("exp_done")
        probs_made, probs_turned, prob_t_made = sem("probs_made"), sem("probs_turned"), sem("prob_t_made")
        att_done, att_hi, att_ready = sem("att_done"), sem("att_hi"), sem("att_ready")
        hist_zero = sem("hist_zero")
        new_rows_made = sem("new_rows_made")
        d_made = sem("d_made")
        z_made = sem("z_made")
        pool_done, pool_hi, pool_ready = sem("pool_done"), sem("pool_hi"), sem("pool_ready")
        conv_made, conv_hi, conv_ready = sem("conv_made"), sem("conv_hi"), sem("conv_ready")
        state_in, const_in, x_in = sem("state_in"), sem("const_in"), sem("x_in")
        stored, kv_stored, y_stored = sem("stored"), sem("kv_stored"), sem("y_stored")
        zeroed, consts_made = sem("zeroed"), sem("consts_made")
        passed = sem("passed")
        x_turned, x_copied = sem("x_turned"), sem("x_copied")
        out_turned, out_act, out_dve = sem("out_turned"), sem("out_act"), sem("out_dve")

        def alone(eng):
            eng.sem_inc(passed, 1)

        class Own:

            def __init__(self, eng, sem_):
                self.eng, self.sem, self.base, self.n, self.outer = eng, sem_, 0, 0, []

            def inc(self, ins):
                ins.then_inc(self.sem, 1)
                self.n += 1

            def wait(self, back=0):
                self.eng.wait_ge(self.sem, self.base + self.n - back)

            def loop(self, i, steps):
                self.outer.append((self.base, self.n, steps))
                self.base, self.n = self.base + self.n + i * steps, 0

            def end(self, times):
                base_, n, steps = self.outer.pop()
                assert self.n == steps, (self.n, steps)
                self.base, self.n = base_, n + times * steps

        def tile(t, k, hf=None):
            return t[:, k * NT:(k + 1) * NT] if hf is None else t[:, k * NT + hf * HT:k * NT + hf * HT + HT]

        def at_tile(t, k, hf):
            return t[:, ds(k * NT + hf * HT, HT)]

        def bank(b, n=HT):
            return ps[:, b, 0:n]

        def f32(ap):
            return ap.bitcast(F32)

        def pcol(l, c):
            return prm[:, ds(l * NPC + c, 1)]

        def gcol(l, n, k):
            return pcol(l, PC_G + n * KD + k)

        def ext_parts(buf, t, hist, width, hf):
            o = t * width
            if hf == 0:
                return [(buf[:, o + hist:o + hist + HT], slice(0, HT), None)]
            smp = buf[:, o + hist + SEQ:o + width].rearrange("p (b t) -> p b t", b=DEC_B)[:, :, hist:hist + DEC_T]
            return [(buf[:, o + hist + HT:o + hist + SEQ], slice(0, HP), None), (smp, slice(HP, HT), DEC_B)]

        def q_parts(j, hf):
            pr = q_t[:, 0:NG * SEQ].rearrange("p (c j t) -> p c j t", j=NG, t=CHUNK)[:, :, j]
            if hf == 0:
                return [(pr[:, 0:HT // CHUNK], slice(0, HT), HT // CHUNK)]
            sm = q_t[:, NG * SEQ:].rearrange("p (b j t) -> p b j t", j=NG, t=DEC_T)[:, :, j]
            return [(pr[:, HT // CHUNK:], slice(0, HP), HP // CHUNK), (sm, slice(HP, HT), DEC_B)]

        def cut(ap, sl, b):
            ap = ap[:, sl]
            return ap if b is None else ap.rearrange("p (b t) -> p b t", b=b)

        def steps_of(i):
            return ("p", i, CHUNK if i == 0 else WIN) if i < SEQ // CHUNK else ("s", 4 * (i - SEQ // CHUNK), KEYS_S)

        def const_loads():
            out = [(ident[:, :], c_ident), (ones[:, :], c_ones), (count[:, :], c_count)]
            for l in range(DEPTH):
                dst = prm_rows[:, l * P:(l + 1) * P]
                out += [(dst[PC_G:PC_BG], norm_g[l].rearrange("n (k p) -> (n k) p", p=P)),
                        (dst[PC_BG:PC_PS], b_gate[l].rearrange("(k p) -> k p", p=P)),
                        (dst[PC_PS:PC_WC], pool_scale[l].rearrange("(k p) -> k p", p=P)),
                        (dst[PC_WC:NPC], w_conv[l].rearrange("j (k p) -> (j k) p", p=P))]
            for e in range(2):
                out.append((sink_p[HD * e:HD * e + HD, :].rearrange("p (l a) -> p l a", l=DEPTH),
                            sinks.rearrange("l (a e) -> e l a", e=2)[e:e + 1].to_broadcast([HD, DEPTH, 4])))
            for hd in range(NH):
                out.append((sink_s[DEC_T * hd:DEC_T * hd + DEC_T, :],
                            sinks.rearrange("l h -> h l")[hd:hd + 1].to_broadcast([DEC_T, DEPTH])))
            for q in range(2):
                dst = wp[HD * q:HD * q + HD, :].rearrange("p (a q c) -> p a q c", q=2, c=HD)[:, :, q, :]
                out.append((dst, w_pool.rearrange("l (t q) c d -> q c (l t) d", q=2)[q]))
            return out

        block = ctx.enter_context(nc.Block())

        @block.sync
        def _(sp):
            for b in range(4):
                sp.dma_start(rows[:, b * D:(b + 1) * D], x_prompt[0, b * P:(b + 1) * P, :]).then_inc(x_in, 16)
            sp.dma_start(rows[:, 4 * D:5 * D], x_sample.rearrange("b t d -> (b t) d")).then_inc(x_in, 16)

            def load(pair, slot, parts):
                sp.wait_ge(w_split, 2 * pair + slot + 1)
                alone(sp)
                assert len(parts) == LOADS
                for dst, src in parts:
                    sp.dma_start(dst, src).then_inc(raw_loaded[slot], 16)

            def columns(w, l, row0, nk, col, slot):
                src = w[ds(l, 1)].rearrange("a (k p) c -> p (a k) c", p=P)[:, row0 // P:row0 // P + nk, :]
                dst = raw[slot][:, 0:nk * P].rearrange("p (k c) -> p k c", c=P)
                q = (nk + LOADS - 1) // LOADS
                return [(dst[:, a:min(a + q, nk)], src[:, a:min(a + q, nk), ds(col, P)]) for a in range(0, nk, q)]

            def gate_up(pair, n, l, f):
                for s in range(2):
                    load(pair, s, columns(w_ffn[n][s], l, 0, KD, f * P, s))

            def q_columns(l, j, slot):
                src = w_in[ds(l, 1)].rearrange("a (k p) c -> p (a k) c", p=P)
                dst = raw[slot][:, 0:KD * P].rearrange("p (k c) -> p k c", c=P)
                out = []
                for g in range(2):
                    c0 = COL_Q + HD * (NG * g + j)
                    for a in range(0, KD, 4):
                        out.append((dst[:, a:a + 4, HD * g:HD * g + HD], src[:, a:a + 4, c0:c0 + HD]))
                return out

            def branch_rows(l, m, slot):
                src = w_branch[ds(l, 1)].rearrange("a r c -> (a r) c")[:, ds(m * P, P)]
                dst = raw[slot][:, 0:KD * P].rearrange("p (k c) -> p k c", c=P)
                a0, a1 = PW, PW + NH * HD
                return [
                    (dst[:, 0:2], src[0:a0].rearrange("(k p) c -> p k c", p=P)),
                    (dst[0:HD, 2:6], src[a0:a0 + NG * HD].rearrange("(k p) c -> p k c", p=HD)),
                    (dst[HD:P, 2:6], src[a0 + NG * HD:a1].rearrange("(k p) c -> p k c", p=HD)),
                    (dst[:, 6:8], src[a1:a1 + CW].rearrange("(k p) c -> p k c", p=P)),
                ]

            def ffn(n, l, first):
                for g in range(2):
                    pair = l * PAIRS + FFN_PAIR0[n] + (FG + KD // 2) * g
                    with sp.Fori(1 if first and g == 0 else 0, FG) as f:
                        gate_up(pair + f, n, l, f + g * FG)
                    with sp.Fori(0, KD // 2) as i:
                        for s in range(2):
                            load(pair + FG + i, s, columns(w_ffn[n][2], l, g * FG * P, FG, (2 * i + s) * P, s))

            gate_up(0, 0, 0, 0)
            with sp.Fori(0, DEPTH) as l:
                ffn(0, l, True)
                pair = l * PAIRS + MIX_PAIR0
                load(pair, 0, columns(w_in, l, 0, KD, COL_K, 0))
                load(pair, 1, columns(w_in, l, 0, KD, COL_V, 1))
                for j in range(4):
                    load(pair + 1 + j // 2, j % 2, q_columns(l, j, j % 2))
                for i, cols in enumerate(((COL_P, COL_P + P), (COL_XC, COL_CG), (COL_XC + P, COL_CG + P),
                                          (COL_BG, COL_BG + P))):
                    for s in range(2):
                        load(pair + 3 + i, s, columns(w_in, l, 0, KD, cols[s], s))
                with sp.Fori(0, KD) as m:
                    pm = pair + MIX_PROJ + 2 * m
                    load(pm, 0, columns(w_in, l, 0, KD, COL_GATE + m * P, 0))
                    load(pm, 1, columns(w_in, l, 0, KD, COL_GATE + D + m * P, 1))
                    load(pm + 1, 0, columns(w_in, l, 0, KD, COL_GATE + 2 * D + m * P, 0))
                    load(pm + 1, 1, branch_rows(l, m, 1))
                with sp.Fori(0, KD // 2) as i:
                    for s in range(2):
                        load(pair + MIX_PROJ + 2 * KD + i, s, columns(w_out, l, 0, KD, (2 * i + s) * P, s))
                ffn(1, l, False)
                gate_up((l + 1) * PAIRS, 0, (l + 1) % DEPTH, 0)

            for b in range(5):
                sp.wait_ge(out_act, b + 1)
                sp.wait_ge(out_dve, b + 1)
                dst = o_yp[0, b * P:(b + 1) * P, :] if b < 4 else o_ys.rearrange("b t d -> (b t) d")
                sp.dma_start(dst, rows[:, b * D:(b + 1) * D]).then_inc(y_stored, 16)
            sp.wait_ge(y_stored, 16 * 5)

        @block.tensor
        def _(pe):
            def dots(out, w, s, k0, x, ks, hf, first, last):
                xh, xl = x
                for n, (kw, kx) in enumerate(ks):
                    wh, wl = (t[s][:, kw * P:(kw + 1) * P] for t in (w_hi, w_lo))
                    pe.matmul(out, wh, tile(xh, kx, hf), start=first and n == 0, stop=False)
                    pe.matmul(out, wh, tile(xl, kx, hf), start=False, stop=False)
                    mm = pe.matmul(out, wl, tile(xh, kx, hf), start=False, stop=last and n == len(ks) - 1)
                return mm

            def stat(acc, b, squares):
                pe.wait_ge(sq_added, squares)
                pe.matmul(bank(b), ones[:, :], acc[:, :], start=True, stop=True).then_inc(stat_done, 1)

            def group(pair, g, s, b, x, ks, hf, ready=None, insert=None):
                pe.wait_ge(w_split, 2 * pair + s + 3)
                pe.wait_ge(evac, g + 1)
                cuts = [ks[i:i + 1] for i in range(len(ks))] if ready is not None else [ks[:4], ks[4:]]
                if insert is None and ready is None:
                    cuts = [ks]
                for i, part in enumerate(cuts):
                    if ready is not None:
                        pe.wait_ge(ready[0], ready[1] + i)
                    mm = dots(bank(b), (w_hi, w_lo), s, 0, x, part, hf, i == 0, i == len(cuts) - 1)
                    if insert is not None and i == (3 if ready is not None else 0):
                        insert()
                mm.then_inc(group_done, 1)

            K8 = [(k, k) for k in range(KD)]
            KF = [(k, k) for k in range(FG)]

            def pair_groups(pair, g, x, ks, ready=None, inserts=(None,) * 4):
                for q in range(4):
                    hf = q // 2
                    rd = None if ready is None else ready[hf] if q % 2 == 0 else None
                    group(pair, g + q, q % 2, q, x, ks, hf, rd, inserts[q])

            def first_pair(pair, g, n):
                base_sq = SQUARES * n + 2
                pair_groups(pair, g, (x_hi, x_lo), K8,
                            ready=((x_ready, 16 * n + 1), (x_ready, 16 * n + 9)),
                            inserts=(lambda: stat(acc_y[1], BY[1], base_sq + 19),
                                     lambda: stat(acc_x[0], BX[0], base_sq + 24),
                                     None,
                                     lambda: stat(acc_x[1], BX[1], base_sq + 32)))

            def last_pair(pair, g, n, x, ks):
                pair_groups(pair, g, x, ks,
                            inserts=(None, None, lambda: stat(acc_y[0], BY[0], SQUARES * (n + 1) + 2 + 14), None))

            def ffn(n, l, seam):
                for fg in range(2):
                    pair = l * PAIRS + FFN_PAIR0[n] + (FG + KD // 2) * fg
                    g = l * GROUPS + FFN_GROUP0[n] + 4 * (FG + KD // 2) * fg
                    if fg == 0:
                        first_pair(pair, g, seam)
                    with pe.Fori(1 - fg, FG) as f:
                        pair_groups(pair + f, g + 4 * f, (x_hi, x_lo), K8)
                    unit = 2 + l * 8 * FG + n * 4 * FG + fg * 2 * FG

                    def down(i):
                        return pair + FG + i, g + 4 * FG + 4 * i

                    pe.wait_ge(mid_split, unit + 2 * FG - 1)
                    pp, gg = down(0)
                    for q in range(4):
                        if q == 2:
                            pe.wait_ge(mid_split, unit + 2 * FG)
                            alone(pe)
                        group(pp, gg + q, q % 2, q, (mid_hi, mid_lo), KF, q // 2)
                    with pe.Fori(1, KD // 2 - fg) as i:
                        pair_groups(*down(i), (mid_hi, mid_lo), KF)
                    if fg == 1:
                        last_pair(*down(KD // 2 - 1), seam, (mid_hi, mid_lo), KF)

            def turn(dst, src, n=P):
                return pe.transpose(dst, src, ident[0:n, 0:n])

            def att_scores(l, i):
                kind, c, w = steps_of(i)
                if i == 0:
                    pe.wait_ge(evac, l * GROUPS + MIX_GROUP0 + 12 + 4)
                    pe.wait_ge(turned_out, 4 * l + 4)
                if i >= 2:
                    pe.wait_ge(exp_in, l * ATT_STEPS + i - 1)
                alone(pe)
                b = 4 + i % 2
                for g in range(2):
                    hs = slice(HD * g, HD * g + HD)
                    if g == 1:
                        mm.then_inc(scores_half, 1)
                        pe.wait_ge(scores_half, l * ATT_STEPS + i + 1)
                        alone(pe)
                    for j in range(2 if kind == "p" else 4):
                        if kind == "p":
                            q = q_t[hs, (2 * c + j) * P:(2 * c + j + 1) * P]
                            lo = max(0, c - 1) * CHUNK
                            blk = 2 * g + j
                            mm = pe.matmul(ps[:, b, blk * w:blk * w + w], q, k_t[hs, lo:lo + w], start=True, stop=True)
                        else:
                            q = q_t[hs, NG * SEQ + (c + j) * HD:NG * SEQ + (c + j + 1) * HD]
                            mm = pe.matmul(ps[hs, b, j * w:j * w + w], q, k_s[hs, (c + j) * w:(c + j) * w + w],
                                           start=True, stop=True)
                mm.then_inc(scores_done, 1)

            def att_turn(l, i):
                _, _, w = steps_of(i)
                pe.wait_ge(probs_made, l * ATT_STEPS + i + 1)
                if i >= 1:
                    pe.wait_ge(prob_t_made, l * ATT_STEPS + i)
                alone(pe)
                pr = prob[i % 3][:, 0:4 * (w + 1)].rearrange("p (a k) -> p a k", k=w + 1)
                for a in range(4):
                    mm = turn(ps[0:w, 6, a * P:a * P + P], pr[:, a, 0:w])
                mm.then_inc(probs_turned, 1)

            def att_values(l, i):
                kind, c, w = steps_of(i)
                pe.wait_ge(prob_t_made, l * ATT_STEPS + i + 1)
                if i >= 1:
                    pe.wait_ge(att_ready, l * ATT_STEPS + i)
                alone(pe)
                pt = prob_t[i % 2]
                for g in range(2):
                    hs = slice(HD * g, HD * g + HD)
                    if kind == "p":
                        mm = pe.matmul(ps[hs, 7, 0:2 * P], v_win[0:w, c * P + HD * g:c * P + HD * g + HD],
                                       pt[0:w, 2 * P * g:2 * P * g + 2 * P], start=True, stop=True)
                    else:
                        for j in range(4):
                            o = (c + j) * P + HD * g
                            mm = pe.matmul(ps[hs, 7, j * HD:j * HD + HD], v_s[0:w, o:o + HD],
                                           pt[0:w, j * P + HD * g:j * P + HD * g + HD], start=True, stop=True)
                mm.then_inc(att_done, 1)

            def mixer(l, seam):
                pair, g = l * PAIRS + MIX_PAIR0, l * GROUPS + MIX_GROUP0
                x = (x_hi, x_lo)
                first_pair(pair, g, seam)
                group(pair + 1, g + 4, 0, 0, x, K8, 0)
                pe.wait_ge(state_in, 80 * l + 80)
                pe.wait_ge(root_made, 4 * seam + 4)
                for t in range(2):
                    turn(ps[:, 4, 120 * t:120 * t + 120], sp_raw[0:120, t * P:t * P + P], 120)
                for t in range(2):
                    turn(ps[:, 4, 240 + 16 * t:256 + 16 * t], sc_raw[0:16, t * P:t * P + P], 16)
                for t in range(4):
                    mm = turn(ps[:, 5, t * P:t * P + P], k_raw[:, t * P:t * P + P])
                mm.then_inc(turned, 1)
                group(pair + 1, g + 5, 1, 1, x, K8, 0)
                pe.wait_ge(evac, g + 8)
                alone(pe)
                for c in range(8):
                    lo, w = max(0, c - 1) * CHUNK, CHUNK if c == 0 else WIN
                    mm = turn(ps[0:w, 6 + c // 4, (c % 4) * P:(c % 4) * P + P], v_t[:, lo:lo + w])
                mm.then_inc(turned, 1)
                group(pair + 1, g + 6, 0, 2, x, K8, 1)
                group(pair + 1, g + 7, 1, 3, x, K8, 1)
                pe.wait_ge(turned_out, 4 * l + 1)
                turn(ps[:, 4, 0:P], k_t[:, SEQ - P:SEQ])
                turn(ps[:, 4, P:2 * P], k_t[:, SEQ:NT])
                turn(ps[:, 4, 2 * P:3 * P], v_t[:, SEQ:NT]).then_inc(turned, 1)
                group(pair + 2, g + 8, 0, 0, x, K8, 0)
                pe.wait_ge(turned_out, 4 * l + 2)
                for b in range(DEC_B):
                    mm = turn(ps[0:DEC_T, 6 + b // 4, (b % 4) * P:(b % 4) * P + P],
                              v_t[:, SEQ + DEC_T * b:SEQ + DEC_T * b + DEC_T])
                mm.then_inc(turned, 1)
                group(pair + 2, g + 9, 1, 1, x, K8, 0)
                group(pair + 2, g + 10, 0, 2, x, K8, 1)
                group(pair + 2, g + 11, 1, 3, x, K8, 1)
                for i in range(16):
                    if i < ATT_STEPS:
                        att_scores(l, i)
                    if 2 <= i < ATT_STEPS + 2:
                        att_turn(l, i - 2)
                    if 3 <= i < ATT_STEPS + 3:
                        att_values(l, i - 3)
                    if i == 14:
                        pe.wait_ge(d_made, l + 1)
                        pe.wait_ge(att_ready, (l + 1) * ATT_STEPS)
                        for t in range(2):
                            for hf in range(2):
                                mm = pe.matmul(bank(4 + 2 * t + hf), wp_of(l, t), tile(d_pool, t, hf), start=True, stop=True)
                        mm.then_inc(pool_done, 1)
                    group(pair + 3 + i // 4, g + 12 + i, i % 2, i % 4, x, K8, (i % 4) // 2)
                pe.wait_ge(pool_ready, 4 * l + 4)
                pe.wait_ge(new_rows_made, l + 1)
                for t in range(2):
                    o, oc = t * PE_W, t * CE_W
                    turn(ps[:, 4, t * P:t * P + P], p_ext[:, o + PH + SEQ - P:o + PH + SEQ])
                    turn(ps[:, 4, (2 + t) * P:(3 + t) * P], c_ext[:, oc + CH_ + SEQ - P:oc + CH_ + SEQ])
                for t in range(4):
                    mm = turn(ps[:, 5, t * P:t * P + P], new_rows[:, t * P:t * P + P])
                mm.then_inc(turned, 1)
                pe.wait_ge(att_ready, (l + 1) * ATT_STEPS)
                pe.wait_ge(conv_ready, 4 * l + 4)
                alone(pe)
                with pe.Fori(0, KD) as m:
                    pm, gm = pair + MIX_PROJ + 2 * m, g + 4 * MIX_PROJ + 12 * m
                    pair_groups(pm, gm, x, K8)
                    br = (br_hi, br_lo)
                    for hf in range(2):
                        o = 4 + 4 * hf
                        group(pm + 1, gm + o, 0, 0, x, K8, hf)
                        group(pm + 1, gm + o + 1, 1, 1, br, K8[0:2], hf)
                        group(pm + 1, gm + o + 2, 1, 2, br, K8[2:6], hf)
                        group(pm + 1, gm + o + 3, 1, 3, br, K8[6:8], hf)
                po, go = pair + MIX_PROJ + 2 * KD, g + 4 * MIX_PROJ + 12 * KD
                mg = (mg_hi, mg_lo)
                for q in range(4):
                    if q % 2 == 0:
                        pe.wait_ge(mg_ready, 2 * KD * l + 2 * KD - 1 + q // 2)
                    group(po, go + q, q % 2, q, mg, K8, q // 2)
                with pe.Fori(1, KD // 2 - 1) as i:
                    pair_groups(po + i, go + 4 * i, mg, K8)
                last_pair(po + KD // 2 - 1, go + 2 * KD - 4, seam, mg, K8)

            def wp_of(l, t):
                return wp_now[:, t * P:(t + 1) * P]

            pe.wait_ge(const_in, CONST_DMAS * 16)
            pe.nop().then_inc(stat_done, 1)
            for t in range(DEPTH):
                mm = turn(ps[:, 0, t * NPC:t * NPC + NPC], prm_rows[0:NPC, t * P:t * P + P], NPC)
            mm.then_inc(x_turned, 1)
            pe.wait_ge(x_in, 16 * 5)
            for k in range(KD):
                if k >= 3:
                    pe.wait_ge(x_copied, 2 * k - 4)
                for b in range(5):
                    mm = turn(ps[:, 2 + 2 * (k % 3) + b // 4, (b % 4) * P:(b % 4) * P + P], rows[:, b * D + k * P:b * D + k * P + P])
                mm.then_inc(x_turned, 1)
            pe.wait_ge(x_copied, 2 * KD)
            pe.wait_ge(zeroed, 1)

            with pe.Fori(0, DEPTH) as l:
                ffn(0, l, 3 * l)
                mixer(l, 3 * l + 1)
                ffn(1, l, 3 * l + 2)

            end = SQUARES * 3 * DEPTH + 2
            stat(acc_y[1], BY[1], end + 19)
            stat(acc_x[0], BX[0], end + 24)
            stat(acc_x[1], BX[1], end + 32)
            pe.wait_ge(root_made, 4 * 3 * DEPTH + 4)
            pe.wait_ge(h_ready, 16 * (3 * DEPTH + 1))
            for b in range(5):
                if b >= 4:
                    pe.wait_ge(out_act, b - 3)
                    pe.wait_ge(out_dve, b - 3)
                for k in range(KD):
                    mm = turn(ps[:, 2 * (b % 4) + k // 4, (k % 4) * P:(k % 4) * P + P], h[:, k * NT + b * P:k * NT + b * P + P])
                mm.then_inc(out_turned, 1)

        @block.scalar
        def _(act):
            own_ = Own(act, act_step)

            def stage(pair, s, nk, used):
                act.wait_ge(raw_loaded[s], 16 * LOADS * (pair + 1))
                if used is not None:
                    act.wait_ge(group_done, used)
                act.activation(w_hi[s][:, 0:nk * P], raw[s][:, 0:nk * P], ACT.Copy).then_inc(w_hi_made, 1)

            def square(src, q, waits):
                pos, base_q = q
                for s_, v in waits:
                    act.wait_ge(s_, v)
                act.wait_ge(sq_added, base_q + pos + 1)
                if waits:
                    alone(act)
                act.activation(sq[pos % 2][:, :], src, ACT.Square).then_inc(sq_made, 1)

            def x_tile(j, n, gl, gn, base_q, pos):
                k, hf = j % KD, j // KD
                act.wait_ge(h_ready, 16 * n + j + 1)
                alone(act)
                act.activation(tile(x_hi, k, hf), tile(h, k, hf), ACT.Copy, scale=gcol(gl, gn, k)).then_inc(x_hi_made, 1)
                square(tile(h, k, hf), (pos, base_q), ())

            def roots(b, hf, s_index, four):
                act.wait_ge(stat_done, s_index + 1)
                act.activation(root[hf][:, :], bank(b), ACT.Sqrt, scale=(4.0 if four else 1.0) / D,
                               bias=(eps4 if four else eps1)[:, 0:1]).then_inc(root_made, 1)

            def seam(n, y, pair, g, four, gl, gn):
                base_q = SQUARES * (n + 1)
                pos = 12
                for what, j in SEAM_SQ:
                    if what == "y":
                        if j == 2:
                            roots(BY[0], 0, 4 * (n + 1), four)
                            stage(pair + 1, 0, KD, g + 3)
                        square(tile(y, KD - 2 + j % 2, j // 2), (pos, base_q), ((evac, g + j + 5),))
                        if j == 3:
                            stage(pair + 1, 1, KD, g + 4)
                    else:
                        if j == 8:
                            roots(BY[1], 1, 4 * (n + 1) + 1, four)
                        x_tile(j, n + 1, gl, gn, base_q, pos)
                    pos += 1
                roots(BX[0], 0, 4 * (n + 1) + 2, False)
                roots(BX[1], 1, 4 * (n + 1) + 3, False)

            def ffn(n, l, sm, gl, gn):
                for fg in range(2):
                    pair = l * PAIRS + FFN_PAIR0[n] + (FG + KD // 2) * fg
                    g = l * GROUPS + FFN_GROUP0[n] + 4 * (FG + KD // 2) * fg
                    unit = l * 8 * FG + n * 4 * FG + fg * 2 * FG

                    def hidden(f, nk):
                        pf, gf, uf = pair + f, g + 4 * f, unit + 2 * f
                        act.wait_ge(evac, gf + 5)
                        act.activation(silu[0][:, :], scaled[0][:, :], ACT.Silu).then_inc(silu_done, 1)
                        act.wait_ge(mid_made, uf + 1)
                        alone(act)
                        act.activation(at_tile(mid_hi, f, 0), mid[0][:, :], ACT.Copy).then_inc(mid_hi_made, 1)
                        stage(pf + 1, 0, nk, gf + 3)
                        act.wait_ge(evac, gf + 7)
                        act.activation(silu[1][:, :], scaled[1][:, :], ACT.Silu).then_inc(silu_done, 1)
                        stage(pf + 1, 1, nk, gf + 4)
                        act.wait_ge(mid_made, uf + 2)
                        alone(act)
                        act.activation(at_tile(mid_hi, f, 1), mid[1][:, :], ACT.Copy).then_inc(mid_hi_made, 1)

                    with act.Fori(0, FG - 1) as f:
                        hidden(f, KD)
                    hidden(FG - 1, FG)
                    pd, gd = pair + FG, g + 4 * FG
                    with act.Fori(0, KD // 2 - 1) as i:
                        for q in range(4):
                            if fg == 1:
                                square(at_tile(y_ffn, 2 * i + q % 2, q // 2), (q, SQUARES * (sm + 1) + 4 * i),
                                       ((evac, gd + 4 * i + q + 5),))
                            if q >= 2:
                                stage(pd + i + 1, q - 2, FG, gd + 4 * i + q + 1)
                    if fg == 0:
                        for s in range(2):
                            stage(pd + KD // 2, s, KD, gd + 2 * KD - 1 + s)
                    else:
                        seam(sm, y_ffn, pd + KD // 2 - 1, gd + 2 * KD - 4, True, gl, gn)

            def copy(dst, src):
                return act.activation(dst, src, ACT.Copy)

            def mixer(l, sm):
                pair, g = l * PAIRS + MIX_PAIR0, l * GROUPS + MIX_GROUP0
                stage(pair + 1, 0, KD, g + 3)
                stage(pair + 1, 1, KD, g + 4)
                act.wait_ge(turned, 5 * l + 1)
                for t in range(2):
                    dst = p_ext[:, t * PE_W + PH + SEQ:(t + 1) * PE_W].rearrange("p (b t) -> p b t", b=DEC_B)
                    copy(dst[:, :, 0:PH], ps[:, 4, 120 * t:120 * t + 120].rearrange("p (b t) -> p b t", b=DEC_B))
                    dst = c_ext[:, t * CE_W + CH_ + SEQ:(t + 1) * CE_W].rearrange("p (b t) -> p b t", b=DEC_B)
                    copy(dst[:, :, 0:CH_], ps[:, 4, 240 + 16 * t:256 + 16 * t].rearrange("p (b t) -> p b t", b=DEC_B))
                ks3 = k_s[:, :].rearrange("p (b k) -> p b k", k=KEYS_S)
                copy(ks3[:, :, DEC_T:], ps[:, 5, :].rearrange("p (b k) -> p b k", k=CHUNK)).then_inc(turned_out, 1)
                act.wait_ge(turned, 5 * l + 2)
                copy(ks3[:, :, 0:DEC_T], k_t[:, SEQ:NT].rearrange("p (b t) -> p b t", b=DEC_B))
                copy(v_win[0:CHUNK, 0:P], ps[0:CHUNK, 6, 0:P])
                copy(v_win[:, P:4 * P], ps[:, 6, P:4 * P])
                copy(v_win[:, 4 * P:8 * P], ps[:, 7, :]).then_inc(turned_out, 1)
                stage(pair + 2, 0, KD, g + 7)
                stage(pair + 2, 1, KD, g + 8)
                act.wait_ge(turned, 5 * l + 3)
                copy(kv_out[:, :], ps[:, 4, 0:3 * P]).then_inc(turned_out, 1)
                act.wait_ge(turned, 5 * l + 4)
                copy(v_s[0:DEC_T, 0:4 * P], ps[0:DEC_T, 6, :])
                copy(v_s[0:DEC_T, 4 * P:], ps[0:DEC_T, 7, :]).then_inc(turned_out, 1)
                act.wait_ge(turned_out, 4 * l + 4)
                act.dma_start(o_kp[ds(l, 1), 0].rearrange("a r h d -> (a r) (h d)"), kv_out[:, 0:P]).then_inc(kv_stored, 16)
                act.dma_start(o_vp[ds(l, 1), 0].rearrange("a r h d -> (a r) (h d)"), v_win[:, 7 * P:]).then_inc(kv_stored, 16)
                for b in range(DEC_B):
                    for o_, c in ((o_ks, P), (o_vs, 2 * P)):
                        act.dma_start(o_[ds(l, 1), b, WIN - DEC_T:].rearrange("a r h d -> (a r) (h d)"),
                                      kv_out[DEC_T * b:DEC_T * b + DEC_T, c:c + P]).then_inc(kv_stored, 16)
                stage(pair + 3, 0, KD, g + 11)
                stage(pair + 3, 1, KD, g + 12)
                for i in range(16):
                    if 2 <= i < ATT_STEPS + 2:
                        t = i - 2
                        w = steps_of(t)[2]
                        act.wait_ge(probs_turned, l * ATT_STEPS + t + 1)
                        copy(prob_t[t % 2][0:w, :], ps[0:w, 6, :]).then_inc(prob_t_made, 1)
                    if 3 <= i < ATT_STEPS + 3:
                        t = i - 3
                        act.wait_ge(att_done, l * ATT_STEPS + t + 1)
                        copy(*att_views(t, br_hi)).then_inc(att_hi, 1)
                    if i < ATT_STEPS:
                        w = steps_of(i)[2]
                        act.wait_ge(exp_in, l * ATT_STEPS + i + 1)
                        e = prob[i % 3][:, 0:4 * (w + 1)]
                        act.activation(e, e, ACT.Exp).then_inc(exp_done, 1)
                    if i == 13:
                        act.wait_ge(evac, g + 12 + 12 + 4)
                        for n_, (e, hist, width) in enumerate(((p_ext, PH, PE_W), (c_ext, CH_, CE_W))):
                            for t in range(2):
                                smp = e[:, t * width + hist + SEQ:(t + 1) * width].rearrange("p (b t) -> p b t", b=DEC_B)
                                dst = new_rows[:, (2 * n_ + t) * P:(2 * n_ + t + 1) * P].rearrange("p (b t) -> p b t", b=DEC_B)
                                ins = copy(dst, smp[:, :, hist:])
                        ins.then_inc(new_rows_made, 1)
                    if i == 14:
                        act.wait_ge(pool_done, l + 1)
                        alone(act)
                        for t in range(2):
                            for hf in range(2):
                                act.activation(tile(br_hi, t, hf), bank(4 + 2 * t + hf), ACT.Copy,
                                               scale=pcol(l, PC_PS + t)).then_inc(pool_hi, 1)
                    if i >= 13:
                        conv_round(l, i - 13)
                    if i % 4 >= 2:
                        stage(pair + 4 + i // 4, i % 2, KD, g + 13 + i)
                conv_round(l, 3)
                act.wait_ge(turned, 5 * l + 5)
                copy(pc_out[:, 0:4 * P], ps[:, 4, :])
                own_.inc(copy(pc_out[:, 4 * P:], ps[:, 5, :]))
                own_.wait()
                for o_, c, nr in ((o_poolp, 0, PH), (o_convp, 2 * P, CH_)):
                    act.dma_start(o_[ds(l, 1), 0].rearrange("a r c -> (a r) c"),
                                  pc_out[P - nr:P, c:c + 2 * P]).then_inc(stored, 16)
                for b in range(DEC_B):
                    for o_, c, nr in ((o_pools, 4 * P, PH), (o_convs, 6 * P, CH_)):
                        act.dma_start(o_[ds(l, 1), b].rearrange("a r c -> (a r) c"),
                                      pc_out[DEC_T * (b + 1) - nr:DEC_T * (b + 1), c:c + 2 * P]).then_inc(stored, 16)

                def gate(l_, m, jj, u, gg):
                    b = (0, 1, 0, 1, 2, 2)[jj]
                    hf = (0, 0, 1, 1, 0, 1)[jj]
                    act.wait_ge(evac, gg + 5)
                    alone(act)
                    act.activation(sig[2 * b + hf][:, :], scaled[jj % 2][:, :], ACT.Sigmoid,
                                   bias=prm[:, ds(l_ * NPC + PC_BG + b * KD + m, 1)]).then_inc(sig_done, 1)

                def round_merged(m, hf):
                    act.wait_ge(merged, 2 * KD * l + 2 * m + hf + 1)
                    alone(act)
                    copy(at_tile(mg_hi, m, hf), xv[hf][:, :]).then_inc(mg_hi_made, 1)

                with act.Fori(0, KD) as m:
                    pm, gm, u = pair + MIX_PROJ + 2 * m, g + 4 * MIX_PROJ + 12 * m, 6 * KD * l + 6 * m
                    gate(l, m, 0, u, gm)
                    gate(l, m, 1, u, gm + 1)
                    stage(pm + 1, 0, KD, gm + 3)
                    gate(l, m, 2, u, gm + 2)
                    stage(pm + 1, 1, KD, gm + 4)
                    gate(l, m, 3, u, gm + 3)
                    gate(l, m, 4, u, gm + 4)
                    round_merged(m, 0)
                    stage(pm + 2, 0, KD, gm + 9)
                    gate(l, m, 5, u, gm + 8)
                    stage(pm + 2, 1, KD, gm + 12)
                    round_merged(m, 1)
                act.wait_ge(kv_stored, 16 * KV_STORES * (l + 1))
                alone(act)
                po, go = pair + MIX_PROJ + 2 * KD, g + 4 * MIX_PROJ + 12 * KD
                with act.Fori(0, KD // 2 - 1) as i:
                    for q in range(4):
                        square(at_tile(y_mix, 2 * i + q % 2, q // 2), (q, SQUARES * (sm + 1) + 4 * i),
                               ((evac, go + 4 * i + q + 5),))
                        if q >= 2:
                            stage(po + i + 1, q - 2, KD, go + 4 * i + q + 1)
                seam(sm, y_mix, po + KD // 2 - 1, go + 2 * KD - 4, False, l, 4)

            def att_views(t, dst):
                kind, c, w = steps_of(t)
                d3 = dst[:, 2 * NT:6 * NT].rearrange("p (j t) -> p j t", t=NT)
                if kind == "p":
                    return d3[:, :, CHUNK * c:CHUNK * c + CHUNK], ps[:, 7, 0:2 * P].rearrange("p (j t) -> p j t", j=NG)
                t0 = SEQ + DEC_T * c
                return (d3[:, :, t0:t0 + 4 * DEC_T].rearrange("p j (b t) -> p b j t", b=4),
                        ps[:, 7, 0:2 * P].rearrange("p (b j t) -> p b j t", b=4, j=NG))

            def conv_round(l, q):
                act.wait_ge(conv_made, 4 * l + q + 1)
                copy(tile(br_hi, 6 + q % 2, q // 2), xv[q % 2][:, :]).then_inc(conv_hi, 1)

            n_const = 0
            for dst, src in const_loads():
                act.dma_start(dst, src, allow_slow_non_contiguous=True).then_inc(const_in, 16)
                n_const += 1
            assert n_const == CONST_DMAS
            act.wait_ge(const_in, 16 * CONST_DMAS)
            act.wait_ge(zeroed, 1)
            act.wait_ge(x_turned, 1)
            copy(prm[:, :], ps[:, 0, 0:DEPTH * NPC]).then_inc(consts_made, 1)
            for k in range(KD):
                act.wait_ge(x_turned, k + 2)
                b0 = 2 + 2 * (k % 3)
                copy(h[:, k * NT:k * NT + 512], ps[:, b0, :]).then_inc(x_copied, 1)
                copy(h[:, k * NT + 512:(k + 1) * NT], ps[:, b0 + 1, 0:NT - 512]).then_inc(x_copied, 1)
            act.wait_ge(consts_made, 1)
            act.wait_ge(x_copied, 2 * KD)
            act.nop().then_inc(h_ready, 16)
            act.nop().then_inc(sq_made, 16)
            act.nop().then_inc(root_made, 2)
            act.nop().then_inc(sig_done, 2)
            stage(0, 0, KD, None)
            stage(0, 1, KD, None)
            for j in range(16):
                x_tile(j, 0, 0, 0, 0, 16 + j)
            roots(BX[0], 0, 2, False)
            roots(BX[1], 1, 3, False)

            with act.Fori(0, DEPTH) as l:
                own_.loop(l, 1)
                act.dma_start(sp_raw[0:120, :], state_pool[ds(l, 1)].rearrange("a b t c -> (a b t) c")).then_inc(state_in, 16)
                act.dma_start(sc_raw[0:16, :], state_conv[ds(l, 1)].rearrange("a b t c -> (a b t) c")).then_inc(state_in, 16)
                ck = cache_k[ds(l, 1), :, CHUNK:].rearrange("a (i e) r h d -> (a e) r i (h d)", e=2)
                for e in range(2):
                    act.dma_start(k_raw[CHUNK * e:CHUNK * e + CHUNK, :].rearrange("p (i c) -> p i c", c=P), ck[e]).then_inc(state_in, 16)
                act.dma_start(v_s[DEC_T:KEYS_S, :].rearrange("p (b c) -> p b c", c=P),
                              cache_v[ds(l, 1), :, CHUNK:].rearrange("a b r h d -> r (a b) (h d)")).then_inc(state_in, 16)
                for o_, c_ in ((o_ks, cache_k), (o_vs, cache_v)):
                    act.dma_start(o_[ds(l, 1), :, 0:WIN - DEC_T].rearrange("a b r h d -> (a b) (r h d)"),
                                  c_[ds(l, 1), :, DEC_T:].rearrange("a b r h d -> (a b) (r h d)")).then_inc(stored, 16)
                ffn(0, l, 3 * l, l, 2)
                mixer(l, 3 * l + 1)
                ffn(1, l, 3 * l + 2, (l + 1) % DEPTH, 0)
                act.wait_ge(stored, 16 * STORES * (l + 1))
                own_.end(DEPTH)

            for b in range(5):
                act.wait_ge(out_turned, b + 1)
                copy(rows[:, b * D:b * D + 512], ps[:, 2 * (b % 4), :]).then_inc(out_act, 1)

        @block.vector
        def _(dve):
            own_ = Own(dve, dve_step)

            def stage(pair, s, nk):
                dve.wait_ge(w_hi_made, 2 * pair + s + 1)
                dve.tensor_tensor(w_lo[s][:, 0:nk * P], raw[s][:, 0:nk * P], f32(w_hi[s][:, 0:nk * P]),
                                  ALU.subtract).then_inc(w_split, 1)

            def inverse(dst, hf, s_index):
                dve.wait_ge(root_made, s_index + 1)
                dve.reciprocal(dst[hf][:, :], root[hf][:, :]).then_inc(inv_made, 1)

            def x_low(j, n, gl, gn):
                k, hf = j % KD, j // KD
                dve.wait_ge(x_hi_made, 16 * n + j + 1)
                dve.scalar_tensor_tensor(out=tile(x_lo, k, hf), in0=tile(h, k, hf), scalar=gcol(gl, gn, k),
                                         in1=f32(tile(x_hi, k, hf)), op0=ALU.mult, op1=ALU.subtract).then_inc(x_ready, 1)

            def x_chain(js, n, y, pl, pn, gl, gn):
                def times_inv(j):
                    own_.inc(dve.tensor_tensor(tb[j % 3][:, :], tile(y, j % KD, j // KD), inv_y[j // KD][:, :], ALU.mult))

                times_inv(js[0])
                for i, j in enumerate(js):
                    if i + 1 < len(js):
                        times_inv(js[i + 1])
                    own_.wait(1 if i + 1 < len(js) else 0)
                    k, hf = j % KD, j // KD
                    dve.scalar_tensor_tensor(out=tile(h, k, hf), in0=tb[j % 3][:, :], scalar=gcol(pl, pn, k),
                                             in1=tile(h, k, hf), op0=ALU.mult, op1=ALU.add).then_inc(h_ready, 1)
                    if i >= 1:
                        x_low(js[i - 1], n, gl, gn)
                x_low(js[-1], n, gl, gn)

            def take_y(y, i, q, g, add):
                dve.wait_ge(group_done, g + q + 1)
                dst = at_tile(y, 2 * i + q % 2, q // 2)
                if add:
                    dve.wait_ge(evac, g + q + 4)
                    dve.tensor_tensor(dst, bank(q), dst, ALU.add).then_inc(evac, 1)
                else:
                    dve.tensor_copy(dst, bank(q)).then_inc(evac, 1)

            def seam(n, y, add, pair, g, pl, pn, gl, gn):
                a = (n + 1, y, pl, pn, gl, gn)
                take_y(y, KD // 2 - 1, 0, g, add)
                take_y(y, KD // 2 - 1, 1, g, add)
                inverse(inv_y, 0, 4 * (n + 1))
                take_y(y, KD // 2 - 1, 2, g, add)
                stage(pair + 1, 0, KD)
                dve.wait_ge(inv_made, 4 * (n + 1) + 1)
                x_chain(range(0, 3), *a)
                take_y(y, KD // 2 - 1, 3, g, add)
                stage(pair + 1, 1, KD)
                dve.wait_ge(evac, g + 8)
                x_chain(range(3, 8), *a)
                inverse(inv_y, 1, 4 * (n + 1) + 1)
                dve.wait_ge(inv_made, 4 * (n + 1) + 2)
                x_chain(range(8, 16), *a)
                inverse(inv_x, 0, 4 * (n + 1) + 2)
                dve.wait_ge(inv_made, 4 * (n + 1) + 3)

            def second_inverse(n):
                inverse(inv_x, 1, 4 * (n + 1) + 3)
                dve.wait_ge(inv_made, 4 * (n + 1) + 4)

            def ffn(n, l, sm, gl, gn):
                for fg in range(2):
                    pair = l * PAIRS + FFN_PAIR0[n] + (FG + KD // 2) * fg
                    g = l * GROUPS + FFN_GROUP0[n] + 4 * (FG + KD // 2) * fg
                    unit = l * 8 * FG + n * 4 * FG + fg * 2 * FG

                    def hidden(f, nk, first=False):
                        pf, gf, uf = pair + f, g + 4 * f, unit + 2 * f
                        for hf in range(2):
                            if hf == 1 and first:
                                second_inverse(sm - 1)
                            dve.wait_ge(group_done, gf + 2 * hf + 1)
                            dve.tensor_tensor(scaled[hf][:, :], bank(2 * hf), inv_x[hf][:, :], ALU.mult).then_inc(evac, 1)
                            if hf == 1:
                                stage(pf + 1, 0, nk)
                            dve.wait_ge(group_done, gf + 2 * hf + 2)
                            dve.tensor_tensor(up[hf][:, :], bank(2 * hf + 1), inv_x[hf][:, :], ALU.mult).then_inc(evac, 1)
                            if hf == 1:
                                stage(pf + 1, 1, nk)
                            dve.wait_ge(evac, gf + 2 * hf + 6)
                            dve.wait_ge(silu_done, uf + hf + 1)
                            dve.wait_ge(mid_split, uf + hf + 1)
                            dve.tensor_tensor(mid[hf][:, :], silu[hf][:, :], up[hf][:, :], ALU.mult).then_inc(mid_made, 1)

                    if fg == 0:
                        hidden(0, KD, True)
                    with dve.Fori(1 - fg, FG - 1) as f:
                        hidden(f, KD)
                    hidden(FG - 1, FG)
                    pd, gd = pair + FG, g + 4 * FG
                    with dve.Fori(0, KD // 2 - 1) as i:
                        for q in range(4):
                            take_y(y_ffn, i, q, gd + 4 * i, fg == 1)
                            if q >= 2:
                                stage(pd + i + 1, q - 2, FG)
                    if fg == 0:
                        for q in range(4):
                            take_y(y_ffn, KD // 2 - 1, q, gd + 2 * KD - 4, False)
                            if q >= 2:
                                stage(pd + KD // 2, q - 2, KD)
                    else:
                        seam(sm, y_ffn, True, pd + KD // 2 - 1, gd + 2 * KD - 4, l, 2 * 2 * n + 1, gl, gn)

            def take_scaled(dst, b, hf, cols=slice(0, HT), bb=None):
                return dve.tensor_tensor(dst, cut(bank(b), cols, bb), cut(inv_x[hf], cols, bb), ALU.mult)

            def soften_a(l, i):
                kind, c, w = steps_of(i)
                snk = (sink_p if kind == "p" else sink_s4)[:, ds(l * 4, 4)]
                s3 = ps[:, 4 + i % 2, 0:4 * w].rearrange("p (a k) -> p a k", k=w)
                e3 = prob[i % 3][:, 0:4 * (w + 1)].rearrange("p (a k) -> p a k", k=w + 1)
                dve.wait_ge(scores_done, l * ATT_STEPS + i + 1)
                own_.inc(dve.tensor_reduce(row_max[:, :], s3, AX, ALU.max))
                own_.wait()
                own_.inc(dve.scalar_tensor_tensor(out=neg[:, :], in0=row_max[:, :], scalar=SCALE, in1=snk,
                                                  op0=ALU.mult, op1=ALU.max))
                own_.wait()
                if i >= 3:
                    dve.wait_ge(probs_turned, l * ATT_STEPS + i - 2)
                dve.tensor_tensor(e3[:, :, w], snk, neg[:, :], ALU.subtract)
                dve.scalar_tensor_tensor(out=e3[:, :, 0:w], in0=s3, scalar=SCALE,
                                         in1=neg[:, :].rearrange("p (a o) -> p a o", o=1).to_broadcast([P, 4, w]),
                                         op0=ALU.mult, op1=ALU.subtract).then_inc(exp_in, 1)

            def soften_b(l, i):
                _, _, w = steps_of(i)
                e3 = prob[i % 3][:, 0:4 * (w + 1)].rearrange("p (a k) -> p a k", k=w + 1)
                dve.wait_ge(exp_done, l * ATT_STEPS + i + 1)
                own_.inc(dve.tensor_reduce(den[:, :], e3, AX, ALU.add))
                own_.wait()
                own_.inc(dve.reciprocal(rden[:, :], den[:, :]))
                own_.wait()
                dve.tensor_tensor(e3[:, :, 0:w], e3[:, :, 0:w],
                                  rden[:, :].rearrange("p (a o) -> p a o", o=1).to_broadcast([P, 4, w]),
                                  ALU.mult).then_inc(probs_made, 1)

            def att_low(l, t):
                kind, c, w = steps_of(t)
                def v(dst):
                    d3 = dst[:, 2 * NT:6 * NT].rearrange("p (j t) -> p j t", t=NT)
                    if kind == "p":
                        return [d3[:, :, CHUNK * c:CHUNK * c + CHUNK]]
                    t0 = SEQ + DEC_T * c
                    return [d3[:, :, t0 + DEC_T * b:t0 + DEC_T * b + DEC_T] for b in range(4)]
                dve.wait_ge(att_hi, l * ATT_STEPS + t + 1)
                src = ps[:, 7, 0:2 * P]
                srcs = [src.rearrange("p (j t) -> p j t", j=NG)] if kind == "p" else \
                    [src[:, HD * b:HD * b + HD].rearrange("p (j t) -> p j t", j=NG) for b in range(4)]
                for lo, hi, s_ in zip(v(br_lo), v(br_hi), srcs):
                    ins = dve.tensor_tensor(lo, s_, f32(hi), ALU.subtract)
                ins.then_inc(att_ready, 1)

            def conv_low(l, q):
                dve.wait_ge(conv_hi, 4 * l + q + 1)
                dve.tensor_tensor(tile(br_lo, 6 + q % 2, q // 2), xv[q % 2][:, :],
                                  f32(tile(br_hi, 6 + q % 2, q // 2)), ALU.subtract).then_inc(conv_ready, 1)

            def pool_low(l):
                for q in range(4):
                    t, hf = q // 2, q % 2
                    dve.wait_ge(pool_hi, 4 * l + q + 1)
                    dve.scalar_tensor_tensor(out=tile(br_lo, t, hf), in0=bank(4 + 2 * t + hf), scalar=pcol(l, PC_PS + t),
                                             in1=f32(tile(br_hi, t, hf)), op0=ALU.mult, op1=ALU.subtract).then_inc(pool_ready, 1)

            def mixer(l, sm):
                pair, g = l * PAIRS + MIX_PAIR0, l * GROUPS + MIX_GROUP0
                for i in range(12):
                    if i == 2:
                        second_inverse(sm - 1)
                    pq, q = i // 4, i % 4
                    hf = q // 2
                    dve.wait_ge(group_done, g + i + 1)
                    if pq == 0:
                        ins = take_scaled((k_t, v_t)[q % 2][:, hf * HT:hf * HT + HT], q, hf)
                    else:
                        for dst, sl, b in q_parts(2 * (pq - 1) + q % 2, hf):
                            ins = take_scaled(dst, q, hf, sl, b)
                    ins.then_inc(evac, 1)
                    if q >= 2:
                        stage(pair + pq + 1, q - 2, KD)
                dve.tensor_copy(wp_now[:, :], wp[:, ds(l * 2 * P, 2 * P)])
                for i in range(16):
                    if i < ATT_STEPS:
                        soften_a(l, i)
                    if 1 <= i < ATT_STEPS + 1:
                        soften_b(l, i - 1)
                    if 3 <= i < ATT_STEPS + 3:
                        att_low(l, i - 3)
                    if i == 15:
                        pool_low(l)
                    q = i % 4
                    hf, gi = q // 2, g + 12 + i
                    dve.wait_ge(group_done, gi + 1)
                    if i < 4:
                        for dst, sl, b in ext_parts(p_ext, q % 2, PH, PE_W, hf):
                            ins = take_scaled(dst, q, hf, sl, b)
                        ins.then_inc(evac, 1)
                    elif i < 12 and q % 2 == 0:
                        take_scaled(xv[hf][:, :], q, hf).then_inc(evac, 1)
                    elif i < 12:
                        own_.inc(take_scaled(tb[hf][:, :], q, hf))
                        own_.wait()
                        dve.wait_ge(evac, gi + 4)
                        for dst, sl, b in ext_parts(c_ext, (i - 4) // 4, CH_, CE_W, hf):
                            ins = dve.tensor_tensor(dst, cut(tb[hf], sl, b), cut(xv[hf], sl, b), ALU.mult)
                        ins.then_inc(evac, 1)
                    else:
                        t = q % 2
                        take_scaled(tb[t][:, :], q, hf).then_inc(evac, 1)
                        dve.wait_ge(evac, gi + 5)
                        dve.wait_ge(z_made, 2 * l + t + 1)
                        if q >= 2:
                            dve.wait_ge(conv_hi, 4 * l + q - 1)
                        z = (win_a, win_b)[t]
                        if hf == 0:
                            parts = [(z[:, 0:HT], slice(0, HT), None)]
                        else:
                            zs = z[:, CH_ + SEQ:CE_W].rearrange("p (b t) -> p b t", b=DEC_B)[:, :, 0:DEC_T]
                            parts = [(z[:, HT:SEQ], slice(0, HP), None), (zs, slice(HP, HT), DEC_B)]
                        for zz, sl, b in parts:
                            ins = dve.tensor_tensor(cut(xv[t], sl, b), cut(tb[t], sl, b), zz, ALU.mult)
                        ins.then_inc(conv_made, 1)
                    if i >= 13:
                        conv_low(l, i - 13)
                    if q >= 2:
                        stage(pair + 4 + i // 4, q - 2, KD)
                conv_low(l, 3)

                def gate(jj, u, gg, b):
                    hf = (0, 0, 1, 1, 0, 1)[jj]
                    dve.wait_ge(group_done, gg + 1)
                    dve.wait_ge(sig_done, u + jj + 1)
                    take_scaled(scaled[jj % 2][:, :], b, hf).then_inc(evac, 1)

                def merge(hf, gg, r):
                    for b in range(3):
                        dve.wait_ge(group_done, gg + b + 1)
                        if b == 0:
                            dve.wait_ge(sig_done, r[0])
                            if r[2] is not None:
                                dve.wait_ge(*r[2])
                            dve.tensor_tensor(xv[hf][:, :], bank(1), sig[hf][:, :], ALU.mult).then_inc(evac, 1)
                            continue
                        dve.tensor_tensor(tb[b % 2][:, :], bank(1 + b), sig[2 * b + hf][:, :], ALU.mult).then_inc(evac, 1)
                        dve.wait_ge(evac, gg + b + 5)
                        ins = dve.tensor_tensor(xv[hf][:, :], xv[hf][:, :], tb[b % 2][:, :], ALU.add)
                        if b == 1:
                            own_.inc(ins)
                            own_.wait()
                        else:
                            ins.then_inc(merged, 1)

                def merged_low(m, hf):
                    dve.wait_ge(mg_hi_made, 2 * KD * l + 2 * m + hf + 1)
                    dve.tensor_tensor(at_tile(mg_lo, m, hf), xv[hf][:, :], f32(at_tile(mg_hi, m, hf)),
                                      ALU.subtract).then_inc(mg_ready, 1)

                with dve.Fori(0, KD) as m:
                    own_.loop(m, 2)
                    pm, gm, u = pair + MIX_PROJ + 2 * m, g + 4 * MIX_PROJ + 12 * m, 6 * KD * l + 6 * m
                    gate(0, u, gm, 0)
                    gate(1, u, gm + 1, 1)
                    gate(2, u, gm + 2, 2)
                    stage(pm + 1, 0, KD)
                    gate(3, u, gm + 3, 3)
                    stage(pm + 1, 1, KD)
                    gate(4, u, gm + 4, 0)
                    merge(0, gm + 5, (u + 7, None, None))
                    merged_low(m, 0)
                    gate(5, u, gm + 8, 0)
                    stage(pm + 2, 0, KD)
                    merge(1, gm + 9, (u + 8, None, None))
                    stage(pm + 2, 1, KD)
                    merged_low(m, 1)
                    own_.end(KD)
                po, go = pair + MIX_PROJ + 2 * KD, g + 4 * MIX_PROJ + 12 * KD
                with dve.Fori(0, KD // 2 - 1) as i:
                    for q in range(4):
                        take_y(y_mix, i, q, go + 4 * i, False)
                        if q >= 2:
                            stage(po + i + 1, q - 2, KD)
                seam(sm, y_mix, False, po + KD // 2 - 1, go + 2 * KD - 4, l, 3, l, 4)

            dve.memset(acc_y[1][:, :], 0.0)
            for q in range(2):
                off = wp[HD * q:HD * q + HD, :].rearrange("p (a q c) -> p a q c", q=2, c=HD)
                dve.memset(off[:, :, 1 - q, :], 0.0)
            dve.memset(eps1[:, :], EPS)
            dve.memset(eps4[:, :], 4 * EPS)
            dve.nop().then_inc(w_split, 2)
            dve.nop().then_inc(evac, 4)
            dve.nop().then_inc(inv_made, 2)
            dve.wait_ge(const_in, 16 * CONST_DMAS)
            for q in range(4):
                ins = dve.tensor_copy(sink_s4[:, :].rearrange("p (l a) -> p l a", a=4)[:, :, q], sink_s[:, :])
            ins.then_inc(zeroed, 1)
            dve.wait_ge(zeroed, 1)
            stage(0, 0, KD)
            stage(0, 1, KD)
            dve.wait_ge(h_ready, 16)
            for j in range(16):
                x_low(j, 0, 0, 0)
            inverse(inv_x, 0, 2)
            dve.wait_ge(inv_made, 3)

            with dve.Fori(0, DEPTH) as l:
                own_.loop(l, DVE_STEPS)
                ffn(0, l, 3 * l, l, 2)
                mixer(l, 3 * l + 1)
                ffn(1, l, 3 * l + 2, (l + 1) % DEPTH, 0)
                own_.end(DEPTH)

            for b in range(5):
                dve.wait_ge(out_turned, b + 1)
                dve.tensor_copy(rows[:, b * D + 512:(b + 1) * D], ps[:, 2 * (b % 4) + 1, :]).then_inc(out_dve, 1)

        @block.gpsimd
        def _(pool):
            own_ = Own(pool, pool_step)

            def add_square(acc, q, pos):
                pool.wait_ge(sq_made, q + pos + 1)
                pool.wait_ge(sq_added, q + pos + 2)
                pool.tensor_tensor(acc[:, :], acc[:, :], sq[pos % 2][:, :], ALU.add).then_inc(sq_added, 1)

            def clear(acc, s_index):
                pool.wait_ge(stat_done, s_index + 1)
                alone(pool)
                own_.inc(pool.memset(acc[:, :], 0.0))

            def seam(n):
                q = SQUARES * (n + 1)
                for i, (what, j) in enumerate(SEAM_SQ):
                    add_square(acc_y[j // 2] if what == "y" else acc_x[j // KD], q, 12 + i)
                clear(acc_y[0], 4 * (n + 1))
                clear(acc_y[1], 4 * (n + 1) + 1)
                clear(acc_x[0], 4 * (n + 1) + 2)
                clear(acc_x[1], 4 * (n + 1) + 3)
                own_.wait()
                alone(pool)

            def ffn(n, l, sm):
                for fg in range(2):
                    unit = l * 8 * FG + n * 4 * FG + fg * 2 * FG
                    with pool.Fori(0, FG) as f:
                        for hf in range(2):
                            pool.wait_ge(mid_hi_made, unit + 2 * f + hf + 1)
                            pool.tensor_tensor(at_tile(mid_lo, f, hf), mid[hf][:, :], f32(at_tile(mid_hi, f, hf)),
                                               ALU.subtract).then_inc(mid_split, 1)
                with pool.Fori(0, KD // 2 - 1) as i:
                    for q in range(4):
                        add_square(acc_y[q // 2], SQUARES * (sm + 1) + 4 * i, q)
                seam(sm)

            def mixer(l, sm):
                g = l * GROUPS + MIX_GROUP0
                own_.inc(pool.tensor_copy(wc_now[:, :], prm[:, ds(l * NPC + PC_WC, 6)]))
                for t in range(2):
                    pool.memset(p_ext[:, t * PE_W:t * PE_W + PH], 0.0)
                    own_.inc(pool.memset(c_ext[:, t * CE_W:t * CE_W + CH_], 0.0))
                own_.wait()
                pool.wait_ge(turned_out, 4 * l + 1)
                pool.wait_ge(evac, g + 12 + 8)

                def window(dst, src, back, lo, hi):
                    a = 2 * back - 1
                    own_.inc(pool.tensor_tensor(dst[lo:hi, a:PE_W], src[lo:hi, a:PE_W],
                                                src[lo:hi, a - back:PE_W - back], ALU.add))
                    own_.wait()

                for t in range(2):
                    src = p_ext[:, t * PE_W:(t + 1) * PE_W]
                    if t == 0:
                        window(win_v, src, 1, 0, HD)
                        window(win_a, src, 1, HD, P)
                        window(win_v, win_a, 2, HD, P)
                    else:
                        window(win_a, src, 1, 0, P)
                        window(win_b, win_a, 2, 0, P)
                        window(win_v, win_b, 4, 0, HD)
                        window(win_a, win_b, 4, HD, P)
                        window(win_v, win_a, 8, HD, P)
                    cnt = count[:, t * 17:t * 17 + 17]
                    smp = [b_[:, PH + SEQ:PE_W].rearrange("p (b t) -> p b t", b=DEC_B)[:, :, PH:] for b_ in (win_v, src)]
                    dp = tile(d_pool, t)
                    d_smp = dp[:, SEQ:NT].rearrange("p (b t) -> p b t", b=DEC_B)
                    pool.tensor_tensor(dp[:, 0:16], win_v[:, PH:PH + 16], cnt[:, 0:16], ALU.mult)
                    pool.tensor_scalar(dp[:, 16:SEQ], win_v[:, PH + 16:PH + SEQ], cnt[:, 16:17], 1.0, ALU.mult, ALU.mult)
                    own_.inc(pool.tensor_scalar(d_smp, smp[0], cnt[:, 16:17], 1.0, ALU.mult, ALU.mult))
                    own_.wait()
                    pool.tensor_tensor(dp[:, 0:SEQ], dp[:, 0:SEQ], src[:, PH:PH + SEQ], ALU.subtract)
                    ins = pool.tensor_tensor(d_smp, d_smp, smp[1], ALU.subtract)
                    if t == 1:
                        ins.then_inc(d_made, 1)
                n = CE_W - 2
                for t in range(2):
                    z, term = (win_a, win_b)[t][:, 0:n], win_v[:, 0:n]
                    src = c_ext[:, t * CE_W:(t + 1) * CE_W]

                    def times(dst, j):
                        return pool.tensor_scalar(dst, src[:, j:n + j], wc_now[:, 2 * j + t:2 * j + t + 1], 1.0, ALU.mult, ALU.mult)

                    if t == 1:
                        pool.wait_ge(z_made, 2 * l + 1)
                    pool.wait_ge(evac, g + 16 + 4 * t + 8)
                    alone(pool)
                    times(z, 0)
                    own_.inc(times(term, 1))
                    own_.wait()
                    own_.inc(pool.tensor_tensor(z, z, term, ALU.add))
                    own_.wait()
                    alone(pool)
                    own_.inc(times(term, 2))
                    own_.wait()
                    pool.tensor_tensor(z, z, term, ALU.add).then_inc(z_made, 1)
                with pool.Fori(0, KD // 2 - 1) as i:
                    for q in range(4):
                        add_square(acc_y[q // 2], SQUARES * (sm + 1) + 4 * i, q)
                seam(sm)

            for a in (acc_x[0], acc_x[1], acc_y[0]):
                own_.inc(pool.memset(a[:, :], 0.0))
            pool.nop().then_inc(mid_split, 2)
            pool.nop().then_inc(sq_added, 18)
            own_.wait()
            for j in range(16):
                add_square(acc_x[j // KD], 0, 16 + j)
            clear(acc_x[0], 2)
            clear(acc_x[1], 3)
            own_.wait()
            with pool.Fori(0, DEPTH) as l:
                own_.loop(l, POOL_STEPS)
                ffn(0, l, 3 * l)
                mixer(l, 3 * l + 1)
                ffn(1, l, 3 * l + 2)
                own_.end(DEPTH)


_INS = ["x_prompt", "x_sample", "state_pool", "state_conv", "cache_k", "cache_v", "norm_g", "ffn1_w_gate",
        "ffn1_w_up", "ffn1_w_down", "w_in", "b_gate", "w_pool", "pool_scale", "sinks", "w_conv", "w_branch",
        "w_out", "ffn2_w_gate", "ffn2_w_up", "ffn2_w_down"]
_OUTS = [(1, SEQ, D), (DEC_B, DEC_T, D), (DEPTH, 1, PH, PW), (DEPTH, 1, CH_, CW), (DEPTH, 1, WIN, NKV, HD),
         (DEPTH, 1, WIN, NKV, HD), (DEPTH, DEC_B, PH, PW), (DEPTH, DEC_B, CH_, CW), (DEPTH, DEC_B, WIN, NKV, HD),
         (DEPTH, DEC_B, WIN, NKV, HD)]


def constants():
    windows = (2, 4, 8, 16)
    cnt = np.zeros((P, 2, 17), np.float32)
    for t in range(2):
        for p in range(P):
            w = windows[2 * t + p // HD]
            cnt[p, t, :16] = 1.0 / np.minimum(np.arange(16) + 1, w)
            cnt[p, t, 16] = 1.0 / w
    return {"c_ident": np.eye(P, dtype=np.float32), "c_ones": np.ones((P, P), np.float32),
            "c_count": cnt.reshape(P, 34)}


def kernel(**inputs):
    import concourse.bacc as _bacc
    from concourse.bass_utils import run_bass_kernel_spmd as _run

    nc = _bacc.Bacc("TRN2", target_bir_lowering=False, num_devices=1, dynamic_dma_scratch_size=1024)
    arrays, args = {}, []
    given = {name: np.ascontiguousarray(inputs[name]) for name in _INS} | constants()
    for name, a in given.items():
        arrays[f"in_{name}_dram"] = a
        args.append(nc.dram_tensor(f"in_{name}_dram", a.shape, F32, kind="ExternalInput").ap())
    for i, shape in enumerate(_OUTS):
        args.append(nc.dram_tensor(f"out_{i}_dram", shape, F32, kind="ExternalOutput").ap())
    trunk_kernel(nc, *args)
    r = _run(nc, [arrays], core_ids=[0])
    return tuple(r.results[0][f"out_{i}_dram"] for i in range(len(_OUTS)))
```

```python
from contextlib import ExitStack

import numpy as np

import concourse.bass as bass
import concourse.mybir as mybir

F32 = mybir.dt.float32
F32R = mybir.dt.float32r
ALU = mybir.AluOpType
ACT = mybir.ActivationFunctionType
AX = mybir.AxisListType.X
ds = bass.ds

P = 128
D = 1024
SEQ, DEC_B, DEC_T = 512, 8, 16
DEPTH = 2
NT = SEQ + DEC_B * DEC_T
HT = NT // 2
HP = SEQ - HT
KD = D // P
FF = 2816
NF = FF // P
FG = NF // 2
CHUNK, HD, NH, NKV = 64, 64, 8, 2
NG = NH // NKV
WIN = 128
PH, CH_ = 15, 2
PW = CW = 256
EPS = 1e-6
SCALE = HD ** -0.5
COL_P, COL_Q, COL_K, COL_V, COL_BG, COL_CG, COL_XC, COL_GATE = 0, 256, 768, 896, 1024, 1280, 1536, 1792
IN_W = COL_GATE + 3 * D
KEYS_S = CHUNK + DEC_T

FFN_PAIRS = 2 * (FG + KD // 2)
MIX_PROJ = 7
MIX_PAIRS = MIX_PROJ + 2 * KD + KD // 2
PAIRS = 2 * FFN_PAIRS + MIX_PAIRS
MIX_GROUPS = 4 * MIX_PROJ + 12 * KD + 2 * KD
GROUPS = 8 * FFN_PAIRS + MIX_GROUPS
FFN_PAIR0 = (0, FFN_PAIRS + MIX_PAIRS)
FFN_GROUP0 = (0, 4 * FFN_PAIRS + MIX_GROUPS)
MIX_PAIR0, MIX_GROUP0 = FFN_PAIRS, 4 * FFN_PAIRS
LOADS = 4

PC_G, PC_BG, PC_PS, PC_WC = 0, 48, 72, 74
NPC = 80

PE_W, CE_W = PH + SEQ + DEC_B * (PH + DEC_T), CH_ + SEQ + DEC_B * (CH_ + DEC_T)
ATT_STEPS = SEQ // CHUNK + 2
ST = 4
SP_ = HT // ST
KV_STORES = 2 + 2 * DEC_B
STORES = 4 + 2 * DEC_B
CONST_DMAS = 1 + 2 + DEC_B + 2
DVE_STEPS = 3 * 20 + 4 * ATT_STEPS + 5 + 2 * KD
POOL_STEPS = 3 * 4 + 3 + 8 + 2 + 6
SQUARES = 32

SEAM_SQ = [("y", 4), ("y", 5), ("y", 6), ("y", 7), ("y", 12), ("x", 0), ("x", 1), ("y", 13), ("x", 2), ("x", 3), ("x", 4),
           ("x", 5), ("y", 14), ("x", 6), ("x", 7), ("y", 15)]
SEAM_SQ_MIX = SEAM_SQ[:13] + [("y", 15), ("x", 6), ("x", 7)]


def trunk_kernel(nc, x_prompt, x_sample, state_pool, state_conv, cache_k, cache_v, norm_g, ffn1_w_gate,
                 ffn1_w_up, ffn1_w_down, w_in, b_gate, w_pool, pool_scale, sinks, w_conv, w_branch, w_out,
                 ffn2_w_gate, ffn2_w_up, ffn2_w_down, c_ident, c_ones, c_count,
                 o_yp, o_ys, o_poolp, o_convp, o_kp, o_vp, o_pools, o_convs, o_ks, o_vs):
    w_ffn = ((ffn1_w_gate, ffn1_w_up, ffn1_w_down), (ffn2_w_gate, ffn2_w_up, ffn2_w_down))
    ctx = ExitStack()
    with ctx:
        base = (nc.sbuf_base + 63) // 64 * 64
        cursor = [base]

        def take(nbytes):
            at = cursor[0]
            cursor[0] += (nbytes + 31) // 32 * 32
            return at

        def view(name, cols, at, dt=F32):
            return nc.alloc_sbuf_tensor_at(name, [P, cols], dt, offset=at)

        def own(name, cols, dt=F32):
            return view(name, cols, take(4 * cols), dt)

        TB = 4 * NT
        at_h, at_x, at_mid, at_y = take(KD * TB), take(2 * KD * TB), take(24 * TB), take(KD * TB)
        h = view("h", KD * NT, at_h)
        x_hi = view("x_hi", KD * NT, at_x, F32R)
        x_lo = view("x_lo", KD * NT, at_x + KD * TB, F32R)
        y_mix = view("y_mix", KD * NT, at_x)
        mid_hi = view("mid_hi", FG * NT, at_mid, F32R)
        mid_lo = view("mid_lo", FG * NT, at_mid + FG * TB, F32R)
        br_hi = view("br_hi", KD * NT, at_mid, F32R)
        br_lo = view("br_lo", KD * NT, at_mid + KD * TB, F32R)
        mg_lo = view("mg_lo", KD * NT, at_mid + 2 * KD * TB, F32R)
        rows = view("rows", 5 * D, at_mid)
        in_mid = [at_mid + 2 * KD * TB]

        def in_mg(name, cols):
            at = in_mid[0]
            in_mid[0] += (4 * cols + 31) // 32 * 32
            return view(name, cols, at)

        p_ext = in_mg("p_ext", 2 * PE_W)
        c_ext = in_mg("c_ext", 2 * CE_W)
        win_a, win_b = in_mg("win_a", PE_W), in_mg("win_b", PE_W)
        assert in_mid[0] <= at_mid + 3 * KD * TB
        y_ffn = view("y_ffn", KD * NT, at_y)
        mg_hi = view("mg_hi", KD * NT, at_y, F32R)
        q_t = view("q_t", 4 * NT, at_y)
        k_t = view("k_t", NT, at_y + 4 * TB)
        v_t = view("v_t", NT, at_y + 5 * TB)
        d_pool = view("d_pool", 2 * NT, at_y + 6 * TB)

        raw = [own(f"raw{s}", FG * P) for s in range(2)]
        w_hi = [own(f"w_hi{s}", FG * P, F32R) for s in range(2)]
        w_lo = [own(f"w_lo{s}", FG * P, F32R) for s in range(2)]
        W8 = 4 * KD * P
        w_first, w_out_last = (
            [[view(f"{n}_{part}{s}", KD * P, at_mid + off + W8 * (2 * s + i), F32R) for s in range(2)]
             for i, part in enumerate(("hi", "lo"))]
            for n, off in (("w_first", 16 * TB - 8 * W8), ("w_out_last", 16 * TB - 4 * W8)))
        assert 16 * TB - 8 * W8 >= 2 * TB and 8 * P <= 4 * 2 * P

        at_tmp = take(8 * 4 * HT + 256)
        scaled = [view(f"scaled{s}", HT, at_tmp + 4 * HT * s) for s in range(2)]
        silu = [view(f"silu{s}", HT, at_tmp + 4 * HT * (2 + s)) for s in range(2)]
        up = [view(f"up{s}", HT, at_tmp + 4 * HT * (4 + s)) for s in range(2)]
        mid = [view(f"mid{s}", HT, at_tmp + 4 * HT * (6 + s)) for s in range(2)]
        w_tail = view("w_tail", 4 * (FG - KD) * P, at_tmp, F32R)
        sig = [view(f"sig{s}", HT, at_tmp + 4 * HT * (2 + s)) for s in range(6)]
        PB = 4 * (WIN + 1) + 4
        prob = [view(f"prob{s}", PB, at_tmp + 4 * PB * s) for s in range(3)]
        prob_t = [view(f"prob_t{s}", 4 * P, at_tmp + 12 * PB + 16 * P * s) for s in range(2)]
        assert 12 * PB + 32 * P <= 8 * 4 * HT + 256

        at_seam = take(12 * 4 * HT)
        sq, diag, low, acc_y, acc_x, tb = (
            [view(f"{n}{s}", HT, at_seam + 4 * HT * (2 * i + s)) for s in range(2)]
            for i, n in enumerate(("sq", "diag", "low", "acc_y", "acc_x", "tb")))
        tb.append(own("tb2", HT))
        v_win = view("v_win", 8 * P, at_seam)
        win_v = view("win_v", PE_W, at_seam + 32 * P)
        assert 32 * P + 4 * PE_W <= 6 * 4 * HT
        inv_x = [own(f"inv_x{s}", HT) for s in range(2)]
        xv = [own(f"xv{s}", HT) for s in range(2)]
        k_s = own("k_s", DEC_B * KEYS_S)
        at_vs = take(4 * DEC_B * P)
        v_s = view("v_s", DEC_B * P, at_vs)
        pc_out = view("pc_out", 8 * P, at_vs)
        at_kr = take(16 * P)
        k_raw = view("k_raw", 4 * P, at_kr)
        prm_rows = view("prm_rows", DEPTH * P, at_kr)
        at_sr = take(4 * (PW + CW))
        sp_raw, sc_raw = view("sp_raw", PW, at_sr), view("sc_raw", CW, at_sr + 4 * PW)
        new_rows = view("new_rows", 4 * P, at_sr)
        kv_out = own("kv_out", 3 * P)
        wp = own("wp", DEPTH * 2 * P)
        wp_now = own("wp_now", 2 * P)
        ident, ones = own("ident", P), own("ones", P)
        count = own("count", 2 * 17)
        prm = own("prm", DEPTH * NPC)
        sink_p, sink_s = own("sink_p", DEPTH * 4), own("sink_s", DEPTH)
        sink_s4 = own("sink_s4", DEPTH * 4)
        row_max, neg, den, rden = own("row_max", 4), own("neg", 4), own("den", 4), own("rden", 4)
        wc_now = own("wc_now", 6)
        root, inv = own("root", 4 * ST), own("inv", 4 * ST)
        eps1, eps4 = own("eps1", 1), own("eps4", 1)
        assert cursor[0] <= nc.sbuf_usable_end, (cursor[0], nc.sbuf_usable_end)
        ctx.enter_context(nc.sbuf_tensor("arena", [P, (cursor[0] - nc.sbuf_base) // 4 - 1], F32))
        ps = ctx.enter_context(nc.psum_tensor("ps", [P, 8, 512], F32))
        BY, BX = (4, 5), (6, 7)
        OUT_BANKS = ((BY[0], BX[0], BX[1]), (0, 1, 2))
        FIRST_BANKS = (BY[0], BX[0])

        def sem(name):
            return ctx.enter_context(nc.semaphore(name))

        raw_loaded = [sem("raw_loaded0"), sem("raw_loaded1")]
        w_hi_made = sem("w_hi_made")
        w_split = sem("w_split")
        group_done = sem("group_done")
        evac = sem("evac")
        silu_done = sem("silu_done")
        mid_made = sem("mid_made")
        mid_hi_made = sem("mid_hi_made")
        mid_split = sem("mid_split")
        sq_made = sem("sq_made")
        sq_added = sem("sq_added")
        sum_done = sem("sum_done")
        root_made = sem("root_made")
        inv_made = sem("inv_made")
        spread_done = sem("spread_done")
        inv_x_made = sem("inv_x_made")
        h_ready = sem("h_ready")
        x_hi_made = sem("x_hi_made")
        x_ready = sem("x_ready")
        sig_done = sem("sig_done")
        merged = sem("merged")
        mg_hi_made = sem("mg_hi_made")
        mg_ready = sem("mg_ready")
        dve_step, pool_step = sem("dve_step"), sem("pool_step")
        turned = sem("turned")
        turned_out = sem("turned_out")
        scores_half = sem("scores_half")
        scores_done = sem("scores_done")
        exp_in = sem("exp_in")
        exp_done = sem("exp_done")
        probs_made = sem("probs_made")
        probs_turned = sem("probs_turned")
        prob_t_made = sem("prob_t_made")
        att_done = sem("att_done")
        att_hi, att_ready = sem("att_hi"), sem("att_ready")
        new_rows_made = sem("new_rows_made")
        pc_made = sem("pc_made")
        d_made = sem("d_made")
        z_made = sem("z_made")
        pool_done = sem("pool_done")
        pool_hi, pool_ready = sem("pool_hi"), sem("pool_ready")
        conv_made = sem("conv_made")
        conv_hi, conv_ready = sem("conv_hi"), sem("conv_ready")
        state_in, const_in, ident_in, prm_in = sem("state_in"), sem("const_in"), sem("ident_in"), sem("prm_in")
        ones_in = sem("ones_in")
        x_in = [sem(f"x_in{b}") for b in range(5)]
        stored, kv_stored, y_stored = sem("stored"), sem("kv_stored"), sem("y_stored")
        zeroed, consts_made = sem("zeroed"), sem("consts_made")
        passed = sem("passed")
        x_turned, prm_turned = sem("x_turned"), sem("prm_turned")
        out_turned, out_act, out_dve = sem("out_turned"), sem("out_act"), sem("out_dve")

        def alone(eng):
            eng.sem_inc(passed, 1)

        class Own:

            def __init__(self, eng, sem_):
                self.eng, self.sem, self.base, self.n, self.outer = eng, sem_, 0, 0, []

            def inc(self, ins):
                ins.then_inc(self.sem, 1)
                self.n += 1

            def wait(self, back=0):
                self.eng.wait_ge(self.sem, self.base + self.n - back)

            def loop(self, i, steps):
                self.outer.append((self.base, self.n, steps))
                self.base, self.n = self.base + self.n + i * steps, 0

            def end(self, times):
                base_, n, steps = self.outer.pop()
                assert self.n == steps, (self.n, steps)
                self.base, self.n = base_, n + times * steps

        def tile(t, k, hf=None):
            return t[:, k * NT:(k + 1) * NT] if hf is None else t[:, k * NT + hf * HT:k * NT + hf * HT + HT]

        def at_tile(t, k, hf):
            return t[:, ds(k * NT + hf * HT, HT)]

        def w_cols(part, where, s, nk):
            if where == "main":
                return [(0, nk, (w_hi, w_lo)[part][s][:, 0:nk * P])]
            if where in ("first", "out_last"):
                return [(0, nk, (w_first if where == "first" else w_out_last)[part][s][:, 0:nk * P])]
            over_x = (x_hi, x_lo)[part][:, 4 * s * NT:4 * (s + 1) * NT].rearrange("p (k t) -> p k t", t=NT)
            o = (2 * s + part) * (FG - KD) * P
            return [(0, KD, over_x[:, :, HT:HT + 2 * P]), (KD, nk, w_tail[:, o:o + (nk - KD) * P])]

        def w_tile(part, where, s, k):
            if where == "x":
                if k < KD:
                    at = (4 * s + k // 2) * NT + HT + (k % 2) * P
                    return (x_hi, x_lo)[part][:, at:at + P]
                o = ((2 * s + part) * (FG - KD) + k - KD) * P
                return w_tail[:, o:o + P]
            return {"main": (w_hi, w_lo), "first": w_first, "out_last": w_out_last}[where][part][s][:, k * P:(k + 1) * P]

        def raw_cols(s, a, z, like):
            r = raw[s][:, a * P:z * P]
            return r.rearrange("p (k c) -> p k c", c=2 * P) if len(like.shape) == 3 else r

        def bank(b, n=HT):
            return ps[:, b, 0:n]

        def f32(ap):
            return ap.bitcast(F32)

        def pcol(l, c):
            return prm[:, ds(l * NPC + c, 1)]

        def gcol(l, n, k):
            return pcol(l, PC_G + n * KD + k)

        def ext_parts(buf, t, hist, width, hf):
            o = t * width
            if hf == 0:
                return [(buf[:, o + hist:o + hist + HT], slice(0, HT), None)]
            smp = buf[:, o + hist + SEQ:o + width].rearrange("p (b t) -> p b t", b=DEC_B)[:, :, hist:hist + DEC_T]
            return [(buf[:, o + hist + HT:o + hist + SEQ], slice(0, HP), None), (smp, slice(HP, HT), DEC_B)]

        def q_parts(j, hf):
            pr = q_t[:, 0:NG * SEQ].rearrange("p (c j t) -> p c j t", j=NG, t=CHUNK)[:, :, j]
            if hf == 0:
                return [(pr[:, 0:HT // CHUNK], slice(0, HT), HT // CHUNK)]
            sm = q_t[:, NG * SEQ:].rearrange("p (b j t) -> p b j t", j=NG, t=DEC_T)[:, :, j]
            return [(pr[:, HT // CHUNK:], slice(0, HP), HP // CHUNK), (sm, slice(HP, HT), DEC_B)]

        def cut(ap, sl, b):
            ap = ap[:, sl]
            return ap if b is None else ap.rearrange("p (b t) -> p b t", b=b)

        def steps_of(i):
            return ("p", i, CHUNK if i == 0 else WIN) if i < SEQ // CHUNK else ("s", 4 * (i - SEQ // CHUNK), KEYS_S)

        def prm_loads():
            out = []
            for l in range(DEPTH):
                dst = prm_rows[:, l * P:(l + 1) * P]
                out += [(dst[PC_G:PC_BG], norm_g[l].rearrange("n (k p) -> (n k) p", p=P)),
                        (dst[PC_BG:PC_PS], b_gate[l].rearrange("(k p) -> k p", p=P)),
                        (dst[PC_PS:PC_WC], pool_scale[l].rearrange("(k p) -> k p", p=P)),
                        (dst[PC_WC:NPC], w_conv[l].rearrange("j (k p) -> (j k) p", p=P))]
            return out

        def const_loads():
            out = [(count[:, :], c_count)]
            for e in range(2):
                out.append((sink_p[HD * e:HD * e + HD, :].rearrange("p (l a) -> p l a", l=DEPTH),
                            sinks.rearrange("l (a e) -> e l a", e=2)[e:e + 1].to_broadcast([HD, DEPTH, 4])))
            for hd in range(NH):
                out.append((sink_s[DEC_T * hd:DEC_T * hd + DEC_T, :],
                            sinks.rearrange("l h -> h l")[hd:hd + 1].to_broadcast([DEC_T, DEPTH])))
            for q in range(2):
                dst = wp[HD * q:HD * q + HD, :].rearrange("p (a q c) -> p a q c", q=2, c=HD)[:, :, q, :]
                out.append((dst, w_pool.rearrange("l (t q) c d -> q c (l t) d", q=2)[q]))
            return out

        block = ctx.enter_context(nc.Block())

        @block.sync
        def _(sp):
            def x_rows(b):
                src = x_prompt[0, b * P:(b + 1) * P, :] if b < 4 else x_sample.rearrange("b t d -> (b t) d")
                sp.dma_start(rows[:, b * D:(b + 1) * D], src).then_inc(x_in[b], 16)

            def load(pair, slot, parts):
                sp.wait_ge(w_split, 2 * pair + slot + 1)
                alone(sp)
                assert len(parts) == LOADS
                for dst, src in parts:
                    sp.dma_start(dst, src).then_inc(raw_loaded[slot], 16)

            def columns(w, l, row0, nk, col, slot):
                src = w[ds(l, 1)].rearrange("a (k p) c -> p (a k) c", p=P)[:, row0 // P:row0 // P + nk, :]
                dst = raw[slot][:, 0:nk * P].rearrange("p (k c) -> p k c", c=P)
                q = (nk + LOADS - 1) // LOADS
                return [(dst[:, a:min(a + q, nk)], src[:, a:min(a + q, nk), ds(col, P)]) for a in range(0, nk, q)]

            def gate_up(pair, n, l, f):
                for s in range(2):
                    load(pair, s, columns(w_ffn[n][s], l, 0, KD, f * P, s))

            def q_columns(l, j, slot):
                src = w_in[ds(l, 1)].rearrange("a (k p) c -> p (a k) c", p=P)
                dst = raw[slot][:, 0:KD * P].rearrange("p (k c) -> p k c", c=P)
                out = []
                for g in range(2):
                    c0 = COL_Q + HD * (NG * g + j)
                    for a in range(0, KD, 4):
                        out.append((dst[:, a:a + 4, HD * g:HD * g + HD], src[:, a:a + 4, c0:c0 + HD]))
                return out

            def branch_rows(l, m, slot):
                src = w_branch[ds(l, 1)].rearrange("a r c -> (a r) c")[:, ds(m * P, P)]
                dst = raw[slot][:, 0:KD * P].rearrange("p (k c) -> p k c", c=P)
                a0, a1 = PW, PW + NH * HD
                return [
                    (dst[:, 0:2], src[0:a0].rearrange("(k p) c -> p k c", p=P)),
                    (dst[0:HD, 2:6], src[a0:a0 + NG * HD].rearrange("(k p) c -> p k c", p=HD)),
                    (dst[HD:P, 2:6], src[a0 + NG * HD:a1].rearrange("(k p) c -> p k c", p=HD)),
                    (dst[:, 6:8], src[a1:a1 + CW].rearrange("(k p) c -> p k c", p=P)),
                ]

            def ffn(n, l, first):
                for g in range(2):
                    pair = l * PAIRS + FFN_PAIR0[n] + (FG + KD // 2) * g
                    with sp.Fori(2 if first and g == 0 else 0, FG) as f:
                        gate_up(pair + f, n, l, f + g * FG)
                    with sp.Fori(0, KD // 2) as i:
                        for s in range(2):
                            load(pair + FG + i, s, columns(w_ffn[n][2], l, g * FG * P, FG, (2 * i + s) * P, s))

            for b in range(5):
                x_rows(b)
            gate_up(0, 0, 0, 0)
            gate_up(1, 0, 0, 1)
            loads = const_loads()
            assert len(loads) == CONST_DMAS
            for dst, src in loads:
                sp.dma_start(dst, src, allow_slow_non_contiguous=True).then_inc(const_in, 16)
            with sp.Fori(0, DEPTH) as l:
                ffn(0, l, True)
                pair = l * PAIRS + MIX_PAIR0
                load(pair, 0, columns(w_in, l, 0, KD, COL_K, 0))
                load(pair, 1, columns(w_in, l, 0, KD, COL_V, 1))
                for j in range(4):
                    load(pair + 1 + j // 2, j % 2, q_columns(l, j, j % 2))
                for i, cols in enumerate(((COL_P, COL_P + P), (COL_XC, COL_CG), (COL_XC + P, COL_CG + P),
                                          (COL_BG, COL_BG + P))):
                    for s in range(2):
                        load(pair + 3 + i, s, columns(w_in, l, 0, KD, cols[s], s))
                    if i == 0:
                        sp.wait_ge(turned_out, 4 * l + 4)
                        sp.dma_start(o_kp[ds(l, 1), 0].rearrange("a r h d -> (a r) (h d)"), kv_out[:, 0:P]).then_inc(kv_stored, 16)
                        sp.dma_start(o_vp[ds(l, 1), 0].rearrange("a r h d -> (a r) (h d)"), v_win[:, 7 * P:]).then_inc(kv_stored, 16)
                        for b in range(DEC_B):
                            for o_, c in ((o_ks, P), (o_vs, 2 * P)):
                                sp.dma_start(o_[ds(l, 1), b, WIN - DEC_T:].rearrange("a r h d -> (a r) (h d)"),
                                              kv_out[DEC_T * b:DEC_T * b + DEC_T, c:c + P]).then_inc(kv_stored, 16)
                with sp.Fori(0, KD) as m:
                    pm = pair + MIX_PROJ + 2 * m
                    load(pm, 0, columns(w_in, l, 0, KD, COL_GATE + m * P, 0))
                    load(pm, 1, columns(w_in, l, 0, KD, COL_GATE + D + m * P, 1))
                    load(pm + 1, 0, columns(w_in, l, 0, KD, COL_GATE + 2 * D + m * P, 0))
                    load(pm + 1, 1, branch_rows(l, m, 1))
                sp.wait_ge(pc_made, l + 1)
                for o_, c, nr in ((o_poolp, 0, PH), (o_convp, 2 * P, CH_)):
                    sp.dma_start(o_[ds(l, 1), 0].rearrange("a r c -> (a r) c"),
                                  pc_out[P - nr:P, c:c + 2 * P]).then_inc(stored, 16)
                for b in range(DEC_B):
                    for o_, c, nr in ((o_pools, 4 * P, PH), (o_convs, 6 * P, CH_)):
                        sp.dma_start(o_[ds(l, 1), b].rearrange("a r c -> (a r) c"),
                                      pc_out[DEC_T * (b + 1) - nr:DEC_T * (b + 1), c:c + 2 * P]).then_inc(stored, 16)
                with sp.Fori(0, KD // 2) as i:
                    for s in range(2):
                        load(pair + MIX_PROJ + 2 * KD + i, s, columns(w_out, l, 0, KD, (2 * i + s) * P, s))
                ffn(1, l, False)
                for f in range(2):
                    gate_up((l + 1) * PAIRS + f, 0, (l + 1) % DEPTH, f)

            def out(b, c0, c1):
                dst = o_yp[0, b * P:(b + 1) * P, c0:c1] if b < 4 else o_ys.rearrange("b t d -> (b t) d")[:, c0:c1]
                sp.dma_start(dst, rows[:, b * D + c0:b * D + c1]).then_inc(y_stored, 16)

            for b in range(2):
                sp.wait_ge(out_act, b + 1)
                out(b, 0, D)
            for b in range(2, 5):
                sp.wait_ge(out_act, b + 1)
                out(b, 0, 512)
            sp.wait_ge(out_act, 6)
            out(2, 512, D)
            for b in range(3, 5):
                sp.wait_ge(out_dve, b - 2)
                out(b, 512, D)
            sp.wait_ge(y_stored, 16 * 8)

        @block.tensor
        def _(pe):
            def sums(acc, b, squares):
                pe.wait_ge(sq_added, squares)
                for c in range(ST):
                    mm = pe.matmul(ps[0:SP_, b, c:c + 1], acc[:, c * SP_:(c + 1) * SP_], ones[:, 0:1], start=True, stop=True)
                mm.then_inc(sum_done, 1)

            def spread(b, index):
                pe.wait_ge(inv_made, index + 1)
                pe.matmul(bank(b), ones[0:SP_, :], diag[index % 2][0:SP_, :], start=True, stop=True).then_inc(spread_done, 1)

            def group(pair, g, s, b, x, ks, hf, between=None, where="main"):
                pe.wait_ge(w_split, 2 * pair + s + 3)
                pe.wait_ge(evac, g + 1)
                xh, xl = x
                for k in ks:
                    if between:
                        between(k)
                    wh, wl = (w_tile(part, where, s, k) for part in range(2))
                    pe.matmul(bank(b), wh, tile(xh, k, hf), start=k == ks[0], stop=False)
                    pe.matmul(bank(b), wh, tile(xl, k, hf), start=False, stop=False)
                    mm = pe.matmul(bank(b), wl, tile(xh, k, hf), start=False, stop=k == ks[-1])
                mm.then_inc(group_done, 1)

            K8, KF = range(KD), range(FG)

            def pair_groups(pair, g, x, ks):
                for q in range(4):
                    group(pair, g + q, q % 2, q, x, ks, q // 2)

            def first_four(pair, g, n, after_mixer):
                sq0 = SQUARES * n + 2

                def stand(at):
                    if at == ((0, "lo", 0, 0) if after_mixer else (0, "hi", 1, 1)):
                        sums(acc_y[1], BY[1], sq0 + (22 if after_mixer else 24))
                    if at == ((0, "lo", 1, 2) if after_mixer else (0, "hi", 1, 4)):
                        sums(acc_x[0], BX[0], sq0 + 24)
                    if at == ((0, "all", 2, 0) if after_mixer else (0, "lo", 0, 1)):
                        spread(BY[1], 4 * n + 1)
                    if at == ((0, "all", 2, 4) if after_mixer else (0, "lo", 1, 0)):
                        spread(BX[0], 4 * n + 2)
                    if at == (1, "lo", 0, 0):
                        sums(acc_x[1], BX[1], sq0 + 32)
                    if at == (1, "lo", 1, 2):
                        spread(BX[1], 4 * n + 3)

                for hf in range(2):
                    for part in ("hi", "lo"):
                        for s in range(2):
                            out = bank((s, FIRST_BANKS[s])[hf])
                            if part == "hi":
                                pe.wait_ge(w_split, 2 * pair + s + 3)
                                if hf == 0:
                                    pe.wait_ge(evac, g + s + 1)
                                elif s == 1:
                                    pe.wait_ge(inv_x_made, 2 * n + 1)
                            for k in range(KD):
                                stand((hf, part, s, k))
                                wh, wl = (w_tile(i, "main", s, k) for i in range(2))
                                if part == "hi":
                                    if s == 0:
                                        pe.wait_ge(x_hi_made, 16 * n + 8 * hf + k + 1)
                                    pe.matmul(out, wh, tile(x_hi, k, hf), start=k == 0, stop=False)
                                    pe.matmul(out, wl, tile(x_hi, k, hf), start=False, stop=False)
                                else:
                                    if s == 0:
                                        pe.wait_ge(x_ready, 16 * n + 8 * hf + k + 1)
                                    mm = pe.matmul(out, wh, tile(x_lo, k, hf), start=False, stop=k == KD - 1)
                            if part == "lo":
                                mm.then_inc(group_done, 1)
                    for s in range(2):
                        group(pair + 1, g + 4 * hf + 2 + s, s, 2 + s, (x_hi, x_lo), K8, hf,
                              lambda k: stand((hf, "all", 2 + s, k)), "first")

            def last_four(pair, g, n, x, ks, where):
                long = len(ks) == FG
                for q in range(8):
                    c = q % 4

                    def between(k):
                        if (q, k) == (4, 5):
                            sums(acc_y[0], BY[0], SQUARES * (n + 1) + 2 + 12)
                        if (q, k) == ((4, 9) if long else (5, 1)):
                            spread(BY[0], 4 * (n + 1))

                    group(pair + c // 2, g + q, c % 2, c, x, ks, q // 4, between, "main" if c < 2 else where)

            def ffn(n, l, seam):
                for fg in range(2):
                    pair = l * PAIRS + FFN_PAIR0[n] + (FG + KD // 2) * fg
                    g = l * GROUPS + FFN_GROUP0[n] + 4 * (FG + KD // 2) * fg
                    if fg == 0:
                        first_four(pair, g, seam, n == 1)
                    with pe.Fori(2 - 2 * fg, FG) as f:
                        pair_groups(pair + f, g + 4 * f, (x_hi, x_lo), K8)
                    unit = 2 + l * 8 * FG + n * 4 * FG + fg * 2 * FG

                    def down(i):
                        return pair + FG + i, g + 4 * FG + 4 * i

                    pe.wait_ge(mid_split, unit + 2 * FG - 1)
                    pp, gg = down(0)
                    for q in range(4):
                        if q == 2:
                            pe.wait_ge(mid_split, unit + 2 * FG)
                            alone(pe)
                        group(pp, gg + q, q % 2, q, (mid_hi, mid_lo), KF, q // 2)
                    with pe.Fori(1, KD // 2 - 2 * fg) as i:
                        pair_groups(*down(i), (mid_hi, mid_lo), KF)
                    if fg == 1:
                        last_four(*down(KD // 2 - 2), seam, (mid_hi, mid_lo), KF, "x")

            def turn(dst, src, n=P):
                return pe.transpose(dst, src, ident[0:n, 0:n])

            def att_scores(l, i, g):
                kind, c, w = steps_of(i)
                if g == 1:
                    pe.wait_ge(scores_half, l * ATT_STEPS + i + 1)
                elif i == 0:
                    pe.wait_ge(evac, l * GROUPS + MIX_GROUP0 + 12 + 4)
                    pe.wait_ge(turned_out, 4 * l + 4)
                if g == 0 and i >= 2:
                    pe.wait_ge(exp_in, l * ATT_STEPS + i - 1)
                alone(pe)
                b = 4 + i % 2
                hs = slice(HD * g, HD * g + HD)
                for j in range(2 if kind == "p" else 4):
                    if kind == "p":
                        q = q_t[hs, (2 * c + j) * P:(2 * c + j + 1) * P]
                        lo = max(0, c - 1) * CHUNK
                        blk = 2 * g + j
                        mm = pe.matmul(ps[:, b, blk * w:blk * w + w], q, k_t[hs, lo:lo + w], start=True, stop=True)
                    else:
                        q = q_t[hs, NG * SEQ + (c + j) * HD:NG * SEQ + (c + j + 1) * HD]
                        mm = pe.matmul(ps[hs, b, j * w:j * w + w], q, k_s[hs, (c + j) * w:(c + j) * w + w],
                                       start=True, stop=True)
                mm.then_inc((scores_half, scores_done)[g], 1)

            def att_turn(l, i):
                _, _, w = steps_of(i)
                pe.wait_ge(probs_made, l * ATT_STEPS + i + 1)
                if i >= 1:
                    pe.wait_ge(prob_t_made, l * ATT_STEPS + i)
                alone(pe)
                pr = prob[i % 3][:, 0:4 * (w + 1)].rearrange("p (a k) -> p a k", k=w + 1)
                for a in range(4):
                    mm = turn(ps[0:w, 6, a * P:a * P + P], pr[:, a, 0:w])
                mm.then_inc(probs_turned, 1)

            def att_values(l, i):
                kind, c, w = steps_of(i)
                pe.wait_ge(prob_t_made, l * ATT_STEPS + i + 1)
                if i >= 1:
                    pe.wait_ge(att_ready, l * ATT_STEPS + i)
                alone(pe)
                pt = prob_t[i % 2]
                for g in range(2):
                    hs = slice(HD * g, HD * g + HD)
                    if kind == "p":
                        mm = pe.matmul(ps[hs, 7, 0:2 * P], v_win[0:w, c * P + HD * g:c * P + HD * g + HD],
                                       pt[0:w, 2 * P * g:2 * P * g + 2 * P], start=True, stop=True)
                    else:
                        for j in range(4):
                            o = (c + j) * P + HD * g
                            mm = pe.matmul(ps[hs, 7, j * HD:j * HD + HD], v_s[0:w, o:o + HD],
                                           pt[0:w, j * P + HD * g:j * P + HD * g + HD], start=True, stop=True)
                mm.then_inc(att_done, 1)

            def mixer(l, seam):
                pair, g = l * PAIRS + MIX_PAIR0, l * GROUPS + MIX_GROUP0
                x = (x_hi, x_lo)
                first_four(pair, g, seam, False)
                pe.wait_ge(state_in, 80 * l + 80)
                pe.wait_ge(inv_x_made, 2 * seam + 2)
                pe.wait_ge(evac, g + 9)
                for t in range(2):
                    turn(ps[:, 4, 120 * t:120 * t + 120], sp_raw[0:120, t * P:t * P + P], 120)
                for t in range(2):
                    turn(ps[:, 4, 240 + 16 * t:256 + 16 * t], sc_raw[0:16, t * P:t * P + P], 16)
                for t in range(4):
                    mm = turn(ps[:, 5, t * P:t * P + P], k_raw[:, t * P:t * P + P])
                mm.then_inc(turned, 1)
                group(pair + 2, g + 8, 0, 0, x, K8, 0)
                pe.wait_ge(evac, g + 10)
                alone(pe)
                for c in range(8):
                    lo, w = max(0, c - 1) * CHUNK, CHUNK if c == 0 else WIN
                    mm = turn(ps[0:w, 6 + c // 4, (c % 4) * P:(c % 4) * P + P], v_t[:, lo:lo + w])
                mm.then_inc(turned, 1)
                group(pair + 2, g + 9, 1, 1, x, K8, 0)
                pe.wait_ge(turned_out, 4 * l + 1)
                turn(ps[:, 4, 0:P], k_t[:, SEQ - P:SEQ])
                turn(ps[:, 4, P:2 * P], k_t[:, SEQ:NT])
                turn(ps[:, 4, 2 * P:3 * P], v_t[:, SEQ:NT]).then_inc(turned, 1)
                group(pair + 2, g + 10, 0, 2, x, K8, 1)
                pe.wait_ge(turned_out, 4 * l + 2)
                for b in range(DEC_B):
                    mm = turn(ps[0:DEC_T, 6 + b // 4, (b % 4) * P:(b % 4) * P + P],
                              v_t[:, SEQ + DEC_T * b:SEQ + DEC_T * b + DEC_T])
                mm.then_inc(turned, 1)
                group(pair + 2, g + 11, 1, 3, x, K8, 1)
                for i in range(16):
                    def attention(k):
                        if k == 1 and i < ATT_STEPS:
                            att_scores(l, i, 0)
                        if k == 3 and i < ATT_STEPS:
                            att_scores(l, i, 1)
                        if k == 5 and 2 <= i < ATT_STEPS + 2:
                            att_turn(l, i - 2)
                        if k == 7 and 3 <= i < ATT_STEPS + 3:
                            att_values(l, i - 3)

                    if i == 14:
                        pe.wait_ge(att_ready, (l + 1) * ATT_STEPS)
                        pe.wait_ge(new_rows_made, l + 1)
                        for t in range(2):
                            o, oc = t * PE_W, t * CE_W
                            turn(ps[:, 4, t * P:t * P + P], p_ext[:, o + PH + SEQ - P:o + PH + SEQ])
                            turn(ps[:, 4, (2 + t) * P:(3 + t) * P], c_ext[:, oc + CH_ + SEQ - P:oc + CH_ + SEQ])
                        for t in range(4):
                            mm = turn(ps[:, 5, t * P:t * P + P], new_rows[:, t * P:t * P + P])
                        mm.then_inc(turned, 1)
                    if i == 15:
                        pe.wait_ge(d_made, l + 1)
                        pe.wait_ge(pc_made, l + 1)
                        for t in range(2):
                            for hf in range(2):
                                mm = pe.matmul(bank(4 + 2 * t + hf), wp_of(l, t), tile(d_pool, t, hf), start=True, stop=True)
                        mm.then_inc(pool_done, 1)
                    group(pair + 3 + i // 4, g + 12 + i, i % 2, i % 4, x, K8, (i % 4) // 2,
                          attention)
                with pe.Fori(0, KD) as m:
                    pm, gm = pair + MIX_PROJ + 2 * m, g + 4 * MIX_PROJ + 12 * m
                    pair_groups(pm, gm, x, K8)
                    br = (br_hi, br_lo)
                    for hf in range(2):
                        o = 4 + 4 * hf
                        group(pm + 1, gm + o, 0, 0, x, K8, hf)
                        if hf == 0:
                            pe.wait_ge(pool_ready, 4 * l + 4)
                            pe.wait_ge(conv_ready, 4 * l + 4)
                            alone(pe)
                        group(pm + 1, gm + o + 1, 1, 1, br, K8[0:2], hf)
                        group(pm + 1, gm + o + 2, 1, 2, br, K8[2:6], hf)
                        group(pm + 1, gm + o + 3, 1, 3, br, K8[6:8], hf)
                po, go = pair + MIX_PROJ + 2 * KD, g + 4 * MIX_PROJ + 12 * KD
                mg = (mg_hi, mg_lo)
                for q in range(4):
                    if q % 2 == 0:
                        pe.wait_ge(mg_ready, 2 * KD * l + 2 * KD - 1 + q // 2)
                    group(po, go + q, q % 2, q, mg, K8, q // 2)
                with pe.Fori(1, KD // 2 - 2) as i:
                    pair_groups(po + i, go + 4 * i, mg, K8)
                last_four(po + KD // 2 - 2, go + 2 * KD - 8, seam, mg, K8, "out_last")

            def wp_of(l, t):
                return wp_now[:, t * P:(t + 1) * P]

            pe.nop().then_inc(sum_done, 1)
            pe.nop().then_inc(spread_done, 1)
            pe.wait_ge(ident_in, 16)
            for bs, waits in (((0, 1, 2), False), ((3, 4), True)):
                for b in bs:
                    pe.wait_ge(x_in[b], 16)
                for k in range(KD):
                    if waits:
                        pe.wait_ge(h_ready, k + 1)
                    for n, b in enumerate(bs):
                        mm = turn(ps[:, k, n * P:(n + 1) * P], rows[:, b * D + k * P:b * D + k * P + P])
                    mm.then_inc(x_turned, 1)
                if not waits:
                    pe.wait_ge(prm_in, 16 * 4 * DEPTH)
                    pe.wait_ge(h_ready, DEPTH)
                    for t in range(DEPTH):
                        mm = turn(ps[:, t, 384:384 + NPC], prm_rows[0:NPC, t * P:t * P + P], NPC)
                    mm.then_inc(prm_turned, 1)
                    pe.wait_ge(consts_made, 1)
            pe.wait_ge(h_ready, 2 * KD)
            pe.wait_ge(zeroed, 1)
            pe.wait_ge(ones_in, 16)

            with pe.Fori(0, DEPTH) as l:
                ffn(0, l, 3 * l)
                mixer(l, 3 * l + 1)
                ffn(1, l, 3 * l + 2)

            last = 3 * DEPTH
            sums(acc_y[1], BY[1], SQUARES * last + 2 + 24)
            spread(BY[1], 4 * last + 1)
            sums(acc_x[0], BX[0], SQUARES * last + 2 + 24)
            pe.wait_ge(evac, 4 + DEPTH * GROUPS)
            pe.wait_ge(w_split, 2 * DEPTH * PAIRS + 2 + 4)
            for b in range(2):
                for k in range(KD):
                    mm = turn(ps[:, 2 * b + k // 4, (k % 4) * P:(k % 4) * P + P], h[:, k * NT + b * P:k * NT + b * P + P])
                mm.then_inc(out_turned, 1)
            pe.wait_ge(root_made, 4 * last + 3)
            for c in range(2):
                if c == 1:
                    pe.wait_ge(out_act, 2)
                for k in range(4 * c, 4 * c + 4):
                    pe.wait_ge(h_ready, 16 * last + KD + k + 1)
                    for b in range(2, 5):
                        mm = turn(ps[:, OUT_BANKS[c][b - 2], (k % 4) * P:(k % 4) * P + P],
                                  h[:, k * NT + b * P:k * NT + b * P + P])
                mm.then_inc(out_turned, 1)

        @block.scalar
        def _(act):
            def stage(pair, s, nk, used, where="main"):
                act.wait_ge(raw_loaded[s], 16 * LOADS * (pair + 1))
                if used is not None:
                    act.wait_ge(group_done, used)
                for a, z, dst in w_cols(0, where, s, nk):
                    ins = act.activation(dst, raw_cols(s, a, z, dst), ACT.Copy)
                ins.then_inc(w_hi_made, 1)

            def square(src, q, waits):
                pos, base_q = q
                for s_, v in waits:
                    act.wait_ge(s_, v)
                act.wait_ge(sq_added, base_q + pos + 1)
                if waits:
                    alone(act)
                act.activation(sq[pos % 2][:, :], src, ACT.Square).then_inc(sq_made, 1)

            def x_tile(j, n, gl, gn, base_q, pos):
                k, hf = j % KD, j // KD
                act.wait_ge(h_ready, 16 * n + j + 1)
                alone(act)
                act.activation(tile(x_hi, k, hf), tile(h, k, hf), ACT.Copy, scale=gcol(gl, gn, k)).then_inc(x_hi_made, 1)
                square(tile(h, k, hf), (pos, base_q), ())

            def roots(b, n, r, four):
                act.wait_ge(sum_done, 4 * (n + 1) + r + 1)
                act.activation(root[0:SP_, ST * r:ST * r + ST], ps[0:SP_, b, 0:ST], ACT.Sqrt,
                               scale=(4.0 if four else 1.0) / D,
                               bias=(eps4 if four else eps1)[0:SP_, 0:1]).then_inc(root_made, 1)

            def keep_inv_x(hf, n):
                act.wait_ge(spread_done, 4 * (n + 1) + 2 + hf + 1)
                act.activation(inv_x[hf][:, :], bank(BX[hf]), ACT.Copy).then_inc(inv_x_made, 1)

            def begin(n, gl, gn):
                keep_inv_x(0, n)
                for j in range(8, 16):
                    x_tile(j, n + 1, gl, gn, SQUARES * (n + 1), 16 + j)
                roots(BX[1], n, 3, False)
                keep_inv_x(1, n)

            def seam(n, y, pair, g, nk, where, four, gl, gn):
                base_q = SQUARES * (n + 1)
                pos = 8
                for s in range(2):
                    stage(pair + 1, s, nk, None, where)
                for what, j in SEAM_SQ_MIX if nk == KD else SEAM_SQ:
                    if what == "y":
                        q = j % 4 + 4 * (j // KD)
                        square(tile(y, j % KD, j // KD), (pos, base_q), ((evac, g + q + 5),))
                        if q == 3:
                            roots(BY[0], n, 0, four)
                        if q in (4, 5):
                            stage(pair + 2, q - 4, KD, g + q + 1)
                    else:
                        x_tile(j, n + 1, gl, gn, base_q, pos)
                    pos += 1
                stage(pair + 3, 0, KD, g + 8, "first")
                roots(BY[1], n, 1, four)
                stage(pair + 3, 1, KD, g + 8, "first")
                roots(BX[0], n, 2, False)

            def states(l):
                act.dma_start(sp_raw[0:120, :], state_pool[ds(l, 1)].rearrange("a b t c -> (a b t) c")).then_inc(state_in, 16)
                act.dma_start(sc_raw[0:16, :], state_conv[ds(l, 1)].rearrange("a b t c -> (a b t) c")).then_inc(state_in, 16)
                ck = cache_k[ds(l, 1), :, CHUNK:].rearrange("a (i e) r h d -> (a e) r i (h d)", e=2)
                for e in range(2):
                    act.dma_start(k_raw[CHUNK * e:CHUNK * e + CHUNK, :].rearrange("p (i c) -> p i c", c=P), ck[e]).then_inc(state_in, 16)
                act.dma_start(v_s[DEC_T:KEYS_S, :].rearrange("p (b c) -> p b c", c=P),
                              cache_v[ds(l, 1), :, CHUNK:].rearrange("a b r h d -> r (a b) (h d)")).then_inc(state_in, 16)
                for o_, c_ in ((o_ks, cache_k), (o_vs, cache_v)):
                    act.dma_start(o_[ds(l, 1), :, 0:WIN - DEC_T].rearrange("a b r h d -> (a b) (r h d)"),
                                  c_[ds(l, 1), :, DEC_T:].rearrange("a b r h d -> (a b) (r h d)")).then_inc(stored, 16)

            def ffn(n, l, sm, gl, gn):
                begin(sm - 1, l, 4 * n)
                for fg in range(2):
                    pair = l * PAIRS + FFN_PAIR0[n] + (FG + KD // 2) * fg
                    g = l * GROUPS + FFN_GROUP0[n] + 4 * (FG + KD // 2) * fg
                    unit = l * 8 * FG + n * 4 * FG + fg * 2 * FG

                    def hidden(f, nk):
                        pf, gf, uf = pair + f, g + 4 * f, unit + 2 * f
                        act.wait_ge(evac, gf + 5)
                        act.activation(silu[0][:, :], scaled[0][:, :], ACT.Silu).then_inc(silu_done, 1)
                        act.wait_ge(mid_made, uf + 1)
                        alone(act)
                        act.activation(at_tile(mid_hi, f, 0), mid[0][:, :], ACT.Copy).then_inc(mid_hi_made, 1)
                        stage(pf + 1, 0, nk, gf + 3)
                        act.wait_ge(evac, gf + 7)
                        act.activation(silu[1][:, :], scaled[1][:, :], ACT.Silu).then_inc(silu_done, 1)
                        stage(pf + 1, 1, nk, gf + 4)
                        act.wait_ge(mid_made, uf + 2)
                        alone(act)
                        act.activation(at_tile(mid_hi, f, 1), mid[1][:, :], ACT.Copy).then_inc(mid_hi_made, 1)

                    def hidden_four():
                        for u in range(4):
                            f, hf = u % 2, u // 2
                            act.wait_ge(evac, g + 2 * u + 5)
                            act.activation(silu[u % 2][:, :], scaled[u % 2][:, :], ACT.Silu).then_inc(silu_done, 1)
                            act.wait_ge(mid_made, unit + u + 1)
                            alone(act)
                            act.activation(tile(mid_hi, f, hf), mid[u % 2][:, :], ACT.Copy).then_inc(mid_hi_made, 1)
                            if u == 1:
                                for s in range(2):
                                    stage(pair + 2, s, KD, g + 5 + s)

                    if fg == 0:
                        hidden_four()
                    with act.Fori(2 - 2 * fg, FG - 1) as f:
                        hidden(f, KD)
                    hidden(FG - 1, FG)
                    pd, gd = pair + FG, g + 4 * FG
                    with act.Fori(0, KD // 2 - 1 - fg) as i:
                        for q in range(4):
                            if q >= 2:
                                stage(pd + i + 1, q - 2, FG, gd + 4 * i + q + 1)
                            if fg == 1:
                                square(at_tile(y_ffn, 2 * i + q % 2, q // 2), (q, SQUARES * (sm + 1) + 4 * i),
                                       ((evac, gd + 4 * i + q + 5),))
                    if fg == 0:
                        if n == 0:
                            states(l)
                        for s in range(2):
                            stage(pd + KD // 2, s, KD, gd + 2 * KD - 1 + s)
                    else:
                        seam(sm, y_ffn, pd + KD // 2 - 2, gd + 2 * KD - 8, FG, "x", True, gl, gn)

            def copy(dst, src):
                return act.activation(dst, src, ACT.Copy)

            def mixer(l, sm):
                pair, g = l * PAIRS + MIX_PAIR0, l * GROUPS + MIX_GROUP0
                begin(sm - 1, l, 2)
                stage(pair + 2, 0, KD, g + 5)
                stage(pair + 2, 1, KD, g + 6)
                act.wait_ge(turned, 5 * l + 1)
                for t in range(2):
                    dst = p_ext[:, t * PE_W + PH + SEQ:(t + 1) * PE_W].rearrange("p (b t) -> p b t", b=DEC_B)
                    copy(dst[:, :, 0:PH], ps[:, 4, 120 * t:120 * t + 120].rearrange("p (b t) -> p b t", b=DEC_B))
                    dst = c_ext[:, t * CE_W + CH_ + SEQ:(t + 1) * CE_W].rearrange("p (b t) -> p b t", b=DEC_B)
                    copy(dst[:, :, 0:CH_], ps[:, 4, 240 + 16 * t:256 + 16 * t].rearrange("p (b t) -> p b t", b=DEC_B))
                ks3 = k_s[:, :].rearrange("p (b k) -> p b k", k=KEYS_S)
                copy(ks3[:, :, DEC_T:], ps[:, 5, :].rearrange("p (b k) -> p b k", k=CHUNK)).then_inc(turned_out, 1)
                act.wait_ge(turned, 5 * l + 2)
                copy(ks3[:, :, 0:DEC_T], k_t[:, SEQ:NT].rearrange("p (b t) -> p b t", b=DEC_B))
                copy(v_win[0:CHUNK, 0:P], ps[0:CHUNK, 6, 0:P])
                copy(v_win[:, P:4 * P], ps[:, 6, P:4 * P])
                copy(v_win[:, 4 * P:8 * P], ps[:, 7, :]).then_inc(turned_out, 1)
                act.wait_ge(turned, 5 * l + 3)
                copy(kv_out[:, :], ps[:, 4, 0:3 * P]).then_inc(turned_out, 1)
                act.wait_ge(turned, 5 * l + 4)
                copy(v_s[0:DEC_T, 0:4 * P], ps[0:DEC_T, 6, :])
                copy(v_s[0:DEC_T, 4 * P:], ps[0:DEC_T, 7, :]).then_inc(turned_out, 1)
                stage(pair + 3, 0, KD, g + 11)
                stage(pair + 3, 1, KD, g + 12)
                for i in range(16):
                    if 2 <= i < ATT_STEPS + 2:
                        t = i - 2
                        w = steps_of(t)[2]
                        act.wait_ge(probs_turned, l * ATT_STEPS + t + 1)
                        copy(prob_t[t % 2][0:w, :], ps[0:w, 6, :]).then_inc(prob_t_made, 1)
                    if 3 <= i < ATT_STEPS + 3:
                        t = i - 3
                        act.wait_ge(att_done, l * ATT_STEPS + t + 1)
                        copy(*att_views(t, br_hi)).then_inc(att_hi, 1)
                    if i < ATT_STEPS:
                        w = steps_of(i)[2]
                        act.wait_ge(exp_in, l * ATT_STEPS + i + 1)
                        e = prob[i % 3][:, 0:4 * (w + 1)]
                        act.activation(e, e, ACT.Exp).then_inc(exp_done, 1)
                    if i == 13:
                        act.wait_ge(evac, g + 12 + 12 + 4)
                        for n_, (e, hist, width) in enumerate(((p_ext, PH, PE_W), (c_ext, CH_, CE_W))):
                            for t in range(2):
                                smp = e[:, t * width + hist + SEQ:(t + 1) * width].rearrange("p (b t) -> p b t", b=DEC_B)
                                dst = new_rows[:, (2 * n_ + t) * P:(2 * n_ + t + 1) * P].rearrange("p (b t) -> p b t", b=DEC_B)
                                ins = copy(dst, smp[:, :, hist:])
                        ins.then_inc(new_rows_made, 1)
                    if i == 14:
                        act.wait_ge(turned, 5 * l + 5)
                        copy(pc_out[:, 0:4 * P], ps[:, 4, :])
                        copy(pc_out[:, 4 * P:], ps[:, 5, :]).then_inc(pc_made, 1)
                    if i >= 13:
                        conv_round(l, i - 13)
                    if i % 4 >= 2:
                        stage(pair + 4 + i // 4, i % 2, KD, g + 13 + i)
                conv_round(l, 3)
                act.wait_ge(pool_done, l + 1)
                alone(act)
                for t in range(2):
                    for hf in range(2):
                        act.activation(tile(br_hi, t, hf), bank(4 + 2 * t + hf), ACT.Copy,
                                       scale=pcol(l, PC_PS + t)).then_inc(pool_hi, 1)

                def gate(l_, m, jj, u, gg):
                    b = (0, 1, 0, 1, 2, 2)[jj]
                    hf = (0, 0, 1, 1, 0, 1)[jj]
                    act.wait_ge(evac, gg + 5)
                    alone(act)
                    act.activation(sig[2 * b + hf][:, :], scaled[jj % 2][:, :], ACT.Sigmoid,
                                   bias=prm[:, ds(l_ * NPC + PC_BG + b * KD + m, 1)]).then_inc(sig_done, 1)

                def round_merged(m, hf):
                    act.wait_ge(merged, 2 * KD * l + 2 * m + hf + 1)
                    alone(act)
                    copy(at_tile(mg_hi, m, hf), xv[hf][:, :]).then_inc(mg_hi_made, 1)

                with act.Fori(0, KD) as m:
                    pm, gm, u = pair + MIX_PROJ + 2 * m, g + 4 * MIX_PROJ + 12 * m, 6 * KD * l + 6 * m
                    gate(l, m, 0, u, gm)
                    gate(l, m, 1, u, gm + 1)
                    stage(pm + 1, 0, KD, gm + 3)
                    gate(l, m, 2, u, gm + 2)
                    stage(pm + 1, 1, KD, gm + 4)
                    gate(l, m, 3, u, gm + 3)
                    gate(l, m, 4, u, gm + 4)
                    round_merged(m, 0)
                    stage(pm + 2, 0, KD, gm + 9)
                    gate(l, m, 5, u, gm + 8)
                    stage(pm + 2, 1, KD, gm + 12)
                    round_merged(m, 1)
                act.wait_ge(kv_stored, 16 * KV_STORES * (l + 1))
                alone(act)
                po, go = pair + MIX_PROJ + 2 * KD, g + 4 * MIX_PROJ + 12 * KD
                with act.Fori(0, KD // 2 - 2) as i:
                    for q in range(4):
                        if q >= 2:
                            stage(po + i + 1, q - 2, KD, go + 4 * i + q + 1)
                        square(at_tile(y_mix, 2 * i + q % 2, q // 2), (q, SQUARES * (sm + 1) + 4 * i),
                               ((evac, go + 4 * i + q + 5),))
                seam(sm, y_mix, po + KD // 2 - 2, go + 2 * KD - 8, KD, "out_last", False, l, 4)

            def att_views(t, dst):
                kind, c, w = steps_of(t)
                d3 = dst[:, 2 * NT:6 * NT].rearrange("p (j t) -> p j t", t=NT)
                if kind == "p":
                    return d3[:, :, CHUNK * c:CHUNK * c + CHUNK], ps[:, 7, 0:2 * P].rearrange("p (j t) -> p j t", j=NG)
                t0 = SEQ + DEC_T * c
                return (d3[:, :, t0:t0 + 4 * DEC_T].rearrange("p j (b t) -> p b j t", b=4),
                        ps[:, 7, 0:2 * P].rearrange("p (b j t) -> p b j t", b=4, j=NG))

            def conv_round(l, q):
                act.wait_ge(conv_made, 4 * l + q + 1)
                copy(tile(br_hi, 6 + q % 2, q // 2), xv[q % 2][:, :]).then_inc(conv_hi, 1)

            act.dma_start(ident[:, :], c_ident).then_inc(ident_in, 16)
            for dst, src in prm_loads():
                act.dma_start(dst, src).then_inc(prm_in, 16)
            act.dma_start(ones[:, :], c_ones).then_inc(ones_in, 16)
            act.nop().then_inc(sq_made, 16)
            act.nop().then_inc(root_made, 2)
            act.nop().then_inc(sig_done, 2)
            act.wait_ge(prm_turned, 1)
            for t in range(DEPTH):
                ins = copy(prm[:, t * NPC:(t + 1) * NPC], ps[:, t, 384:384 + NPC])
            ins.then_inc(consts_made, 1)
            act.wait_ge(consts_made, 1)
            for j in range(KD):
                x_tile(j, 0, 0, 0, 0, 16 + j)
                if j == 3:
                    stage(0, 0, KD, None)
                    stage(0, 1, KD, None)
            act.wait_ge(x_turned, 2 * KD)
            stage(1, 0, KD, None, "first")
            stage(1, 1, KD, None, "first")
            act.wait_ge(zeroed, 1)
            roots(BX[0], -1, 2, False)

            with act.Fori(0, DEPTH) as l:
                ffn(0, l, 3 * l, l, 2)
                mixer(l, 3 * l + 1)
                ffn(1, l, 3 * l + 2, (l + 1) % DEPTH, 0)
                act.wait_ge(stored, 16 * STORES * (l + 1))

            for b in range(2):
                act.wait_ge(out_turned, b + 1)
                copy(rows[:, b * D:b * D + D].rearrange("p (a c) -> p a c", c=512), ps[:, 2 * b:2 * b + 2, :]).then_inc(out_act, 1)
            act.wait_ge(out_turned, 3)
            for b in range(2, 5):
                copy(rows[:, b * D:b * D + 512], ps[:, OUT_BANKS[0][b - 2], :]).then_inc(out_act, 1)
            act.wait_ge(out_turned, 4)
            copy(rows[:, 2 * D + 512:3 * D], ps[:, OUT_BANKS[1][0], :]).then_inc(out_act, 1)

        @block.vector
        def _(dve):
            own_ = Own(dve, dve_step)

            def stage(pair, s, nk, where="main"):
                dve.wait_ge(w_hi_made, 2 * pair + s + 1)
                for (a, z, hi), (_, _, lo) in zip(w_cols(0, where, s, nk), w_cols(1, where, s, nk)):
                    ins = dve.tensor_tensor(lo, raw_cols(s, a, z, lo), f32(hi), ALU.subtract)
                ins.then_inc(w_split, 1)

            def inverse(n, r):
                a = inv[0:SP_, ST * r:ST * r + ST]
                dve.wait_ge(root_made, 4 * (n + 1) + r + 1)
                own_.inc(dve.reciprocal(a, root[0:SP_, ST * r:ST * r + ST]))
                own_.wait()
                dve.tensor_tensor(diag[r % 2][0:SP_, :].rearrange("p (c t) -> p c t", c=ST),
                                  ident[0:SP_, 0:SP_].rearrange("p (o t) -> p o t", o=1).to_broadcast([SP_, ST, SP_]),
                                  a.rearrange("p (c o) -> p c o", o=1).to_broadcast([SP_, ST, SP_]),
                                  ALU.mult).then_inc(inv_made, 1)

            def x_low(j, n, gl, gn):
                k, hf = j % KD, j // KD
                dve.wait_ge(x_hi_made, 16 * n + j + 1)
                dve.scalar_tensor_tensor(out=tile(x_lo, k, hf), in0=tile(h, k, hf), scalar=gcol(gl, gn, k),
                                         in1=f32(tile(x_hi, k, hf)), op0=ALU.mult, op1=ALU.subtract).then_inc(x_ready, 1)

            def new_h(js, n, y, pl, pn):
                def times_inv(j):
                    own_.inc(dve.tensor_tensor(tb[j % 3][:, :], tile(y, j % KD, j // KD), bank(BY[j // KD]), ALU.mult))

                if js[0]:
                    dve.wait_ge(h_ready, 16 * n + js[0])
                times_inv(js[0])
                for i, j in enumerate(js):
                    if i + 1 < len(js):
                        if i >= 1:
                            dve.wait_ge(h_ready, 16 * n + j)
                        times_inv(js[i + 1])
                    own_.wait(1 if i + 1 < len(js) else 0)
                    k, hf = j % KD, j // KD
                    dve.scalar_tensor_tensor(out=tile(h, k, hf), in0=tb[j % 3][:, :], scalar=gcol(pl, pn, k),
                                             in1=tile(h, k, hf), op0=ALU.mult, op1=ALU.add).then_inc(h_ready, 1)

            def put_y(dst, q, g, n, add):
                dve.wait_ge(group_done, g + n + 1)
                if add:
                    dve.wait_ge(evac, g + n + 4)
                    dve.tensor_tensor(dst, bank(q), dst, ALU.add).then_inc(evac, 1)
                else:
                    dve.tensor_copy(dst, bank(q)).then_inc(evac, 1)

            def take_y(y, i, q, g, add):
                put_y(at_tile(y, 2 * i + q % 2, q // 2), q, g, q, add)

            def seam(n, y, add, pair, g, nk, where, pl, pn, gl, gn):
                def take(q):
                    put_y(tile(y, KD // 2 + q % 4, q // 4), q % 4, g, q, add)

                def lows(js):
                    for j in js:
                        x_low(j, n + 1, gl, gn)

                a = (n + 1, y, pl, pn)
                stage(pair + 1, 0, nk, where)
                take(0)
                stage(pair + 1, 1, nk, where)
                for q in range(1, 4):
                    take(q)
                inverse(n, 0)
                take(4)
                dve.wait_ge(spread_done, 4 * (n + 1) + 1)
                dve.wait_ge(evac, g + 8)
                new_h(range(0, 3), *a)
                take(5)
                stage(pair + 2, 0, KD)
                new_h(range(3, 8), *a)
                take(6)
                if nk == KD:
                    take(7)
                stage(pair + 2, 1, KD)
                if nk == KD:
                    lows(range(0, 8))
                    inverse(n, 1)
                    stage(pair + 3, 0, KD, "first")
                    inverse(n, 2)
                    stage(pair + 3, 1, KD, "first")
                else:
                    lows(range(0, 3))
                    take(7)
                    lows(range(3, 5))
                    stage(pair + 3, 0, KD, "first")
                    inverse(n, 1)
                    stage(pair + 3, 1, KD, "first")
                    lows(range(5, 8))
                    inverse(n, 2)
                dve.wait_ge(spread_done, 4 * (n + 1) + 2)
                dve.wait_ge(evac, g + 12)
                new_h(range(8, 16), *a)

            def begin(n, gl, gn):
                for j in range(8, 16):
                    x_low(j, n + 1, gl, gn)
                inverse(n, 3)
                dve.wait_ge(inv_x_made, 2 * (n + 1) + 1)

            def second_half(n):
                dve.wait_ge(inv_x_made, 2 * (n + 1) + 2)

            def ffn(n, l, sm, gl, gn):
                begin(sm - 1, l, 4 * n)
                for fg in range(2):
                    pair = l * PAIRS + FFN_PAIR0[n] + (FG + KD // 2) * fg
                    g = l * GROUPS + FFN_GROUP0[n] + 4 * (FG + KD // 2) * fg
                    unit = l * 8 * FG + n * 4 * FG + fg * 2 * FG

                    def scale(dst, b, hf, gi):
                        dve.wait_ge(group_done, gi + 1)
                        dve.tensor_tensor(dst[:, :], bank(b), inv_x[hf][:, :], ALU.mult).then_inc(evac, 1)

                    def multiply(gi, b, u):
                        dve.wait_ge(evac, gi + 5)
                        dve.wait_ge(silu_done, u + 1)
                        dve.wait_ge(mid_split, u + 1)
                        dve.tensor_tensor(mid[b][:, :], silu[b][:, :], up[b][:, :], ALU.mult).then_inc(mid_made, 1)

                    def hidden(f, nk):
                        pf, gf, uf = pair + f, g + 4 * f, unit + 2 * f
                        for hf in range(2):
                            scale(scaled[hf], 2 * hf, hf, gf + 2 * hf)
                            if hf == 1:
                                stage(pf + 1, 0, nk)
                            scale(up[hf], 2 * hf + 1, hf, gf + 2 * hf + 1)
                            if hf == 1:
                                stage(pf + 1, 1, nk)
                            multiply(gf + 2 * hf + 1, hf, uf + hf)

                    def hidden_four():
                        for hf in range(2):
                            if hf == 1:
                                second_half(sm - 1)
                            for f in range(2):
                                b = (FIRST_BANKS if hf == 1 and f == 0 else (2 * f, 2 * f + 1))
                                scale(scaled[f], b[0], hf, g + 4 * hf + 2 * f)
                                scale(up[f], b[1], hf, g + 4 * hf + 2 * f + 1)
                                if hf == 1 and f == 0:
                                    for s in range(2):
                                        stage(pair + 2, s, KD)
                                if hf == 1:
                                    multiply(g + 5 + 2 * f, f, unit + 2 + f)
                            if hf == 0:
                                for f in range(2):
                                    multiply(g + 2 * f + 1, f, unit + f)

                    if fg == 0:
                        hidden_four()
                    with dve.Fori(2 - 2 * fg, FG - 1) as f:
                        hidden(f, KD)
                    hidden(FG - 1, FG)
                    pd, gd = pair + FG, g + 4 * FG
                    with dve.Fori(0, KD // 2 - 1 - fg) as i:
                        for q in range(4):
                            take_y(y_ffn, i, q, gd + 4 * i, fg == 1)
                            if q >= 2:
                                stage(pd + i + 1, q - 2, FG)
                    if fg == 0:
                        for q in range(4):
                            take_y(y_ffn, KD // 2 - 1, q, gd + 2 * KD - 4, False)
                            if q >= 2:
                                stage(pd + KD // 2, q - 2, KD)
                    else:
                        seam(sm, y_ffn, True, pd + KD // 2 - 2, gd + 2 * KD - 8, FG, "x", l, 2 * 2 * n + 1, gl, gn)

            def take_scaled(dst, b, hf, cols=slice(0, HT), bb=None):
                return dve.tensor_tensor(dst, cut(bank(b), cols, bb), cut(inv_x[hf], cols, bb), ALU.mult)

            def soften_a(l, i):
                kind, c, w = steps_of(i)
                snk = (sink_p if kind == "p" else sink_s4)[:, ds(l * 4, 4)]
                s3 = ps[:, 4 + i % 2, 0:4 * w].rearrange("p (a k) -> p a k", k=w)
                e3 = prob[i % 3][:, 0:4 * (w + 1)].rearrange("p (a k) -> p a k", k=w + 1)
                dve.wait_ge(scores_done, l * ATT_STEPS + i + 1)
                own_.inc(dve.tensor_reduce(row_max[:, :], s3, AX, ALU.max))
                own_.wait()
                own_.inc(dve.scalar_tensor_tensor(out=neg[:, :], in0=row_max[:, :], scalar=SCALE, in1=snk,
                                                  op0=ALU.mult, op1=ALU.max))
                own_.wait()
                if i >= 3:
                    dve.wait_ge(probs_turned, l * ATT_STEPS + i - 2)
                dve.tensor_tensor(e3[:, :, w], snk, neg[:, :], ALU.subtract)
                dve.scalar_tensor_tensor(out=e3[:, :, 0:w], in0=s3, scalar=SCALE,
                                         in1=neg[:, :].rearrange("p (a o) -> p a o", o=1).to_broadcast([P, 4, w]),
                                         op0=ALU.mult, op1=ALU.subtract).then_inc(exp_in, 1)

            def soften_b(l, i):
                _, _, w = steps_of(i)
                e3 = prob[i % 3][:, 0:4 * (w + 1)].rearrange("p (a k) -> p a k", k=w + 1)
                dve.wait_ge(exp_done, l * ATT_STEPS + i + 1)
                own_.inc(dve.tensor_reduce(den[:, :], e3, AX, ALU.add))
                own_.wait()
                own_.inc(dve.reciprocal(rden[:, :], den[:, :]))
                own_.wait()
                dve.tensor_tensor(e3[:, :, 0:w], e3[:, :, 0:w],
                                  rden[:, :].rearrange("p (a o) -> p a o", o=1).to_broadcast([P, 4, w]),
                                  ALU.mult).then_inc(probs_made, 1)

            def att_low(l, t):
                kind, c, w = steps_of(t)
                def v(dst):
                    d3 = dst[:, 2 * NT:6 * NT].rearrange("p (j t) -> p j t", t=NT)
                    if kind == "p":
                        return [d3[:, :, CHUNK * c:CHUNK * c + CHUNK]]
                    t0 = SEQ + DEC_T * c
                    return [d3[:, :, t0 + DEC_T * b:t0 + DEC_T * b + DEC_T] for b in range(4)]
                dve.wait_ge(att_hi, l * ATT_STEPS + t + 1)
                src = ps[:, 7, 0:2 * P]
                srcs = [src.rearrange("p (j t) -> p j t", j=NG)] if kind == "p" else \
                    [src[:, HD * b:HD * b + HD].rearrange("p (j t) -> p j t", j=NG) for b in range(4)]
                for lo, hi, s_ in zip(v(br_lo), v(br_hi), srcs):
                    ins = dve.tensor_tensor(lo, s_, f32(hi), ALU.subtract)
                ins.then_inc(att_ready, 1)

            def conv_low(l, q):
                dve.wait_ge(conv_hi, 4 * l + q + 1)
                dve.tensor_tensor(tile(br_lo, 6 + q % 2, q // 2), xv[q % 2][:, :],
                                  f32(tile(br_hi, 6 + q % 2, q // 2)), ALU.subtract).then_inc(conv_ready, 1)

            def pool_low(l):
                for q in range(4):
                    t, hf = q // 2, q % 2
                    dve.wait_ge(pool_hi, 4 * l + q + 1)
                    dve.scalar_tensor_tensor(out=tile(br_lo, t, hf), in0=bank(4 + 2 * t + hf), scalar=pcol(l, PC_PS + t),
                                             in1=f32(tile(br_hi, t, hf)), op0=ALU.mult, op1=ALU.subtract).then_inc(pool_ready, 1)

            def mixer(l, sm):
                pair, g = l * PAIRS + MIX_PAIR0, l * GROUPS + MIX_GROUP0
                begin(sm - 1, l, 2)
                for i in range(12):
                    if i == 4:
                        second_half(sm - 1)
                    if i < 8:
                        what, hf = i % 4, i // 4
                        q = FIRST_BANKS[what] if hf == 1 and what < 2 else what
                    else:
                        what, hf, q = 4 + i % 2, (i - 8) // 2, i - 8
                    dve.wait_ge(group_done, g + i + 1)
                    if what < 2:
                        ins = take_scaled((k_t, v_t)[what][:, hf * HT:hf * HT + HT], q, hf)
                    else:
                        for dst, sl, b in q_parts(what - 2, hf):
                            ins = take_scaled(dst, q, hf, sl, b)
                    ins.then_inc(evac, 1)
                    if i in (4, 5):
                        stage(pair + 2, i - 4, KD)
                    if i >= 10:
                        stage(pair + 3, i - 10, KD)
                dve.wait_ge(const_in, 16 * CONST_DMAS)
                for q in range(4):
                    ins = dve.tensor_copy(sink_s4[:, q:DEPTH * 4:4], sink_s[:, :])
                own_.inc(ins)
                own_.wait()
                dve.tensor_copy(wp_now[:, :], wp[:, ds(l * 2 * P, 2 * P)])
                for i in range(16):
                    if i < ATT_STEPS:
                        soften_a(l, i)
                    if 1 <= i < ATT_STEPS + 1:
                        soften_b(l, i - 1)
                    if 3 <= i < ATT_STEPS + 3:
                        att_low(l, i - 3)
                    q = i % 4
                    hf, gi = q // 2, g + 12 + i
                    dve.wait_ge(group_done, gi + 1)
                    if i < 4:
                        for dst, sl, b in ext_parts(p_ext, q % 2, PH, PE_W, hf):
                            ins = take_scaled(dst, q, hf, sl, b)
                        ins.then_inc(evac, 1)
                    elif i < 12 and q % 2 == 0:
                        take_scaled(xv[hf][:, :], q, hf).then_inc(evac, 1)
                    elif i < 12:
                        own_.inc(take_scaled(tb[hf][:, :], q, hf))
                        own_.wait()
                        dve.wait_ge(evac, gi + 4)
                        for dst, sl, b in ext_parts(c_ext, (i - 4) // 4, CH_, CE_W, hf):
                            ins = dve.tensor_tensor(dst, cut(tb[hf], sl, b), cut(xv[hf], sl, b), ALU.mult)
                        ins.then_inc(evac, 1)
                    else:
                        t = q % 2
                        take_scaled(tb[t][:, :], q, hf).then_inc(evac, 1)
                        dve.wait_ge(evac, gi + 5)
                        dve.wait_ge(z_made, 2 * l + t + 1)
                        if q >= 2:
                            dve.wait_ge(conv_hi, 4 * l + q - 1)
                        z = (win_a, win_b)[t]
                        if hf == 0:
                            parts = [(z[:, 0:HT], slice(0, HT), None)]
                        else:
                            zs = z[:, CH_ + SEQ:CE_W].rearrange("p (b t) -> p b t", b=DEC_B)[:, :, 0:DEC_T]
                            parts = [(z[:, HT:SEQ], slice(0, HP), None), (zs, slice(HP, HT), DEC_B)]
                        for zz, sl, b in parts:
                            ins = dve.tensor_tensor(cut(xv[t], sl, b), cut(tb[t], sl, b), zz, ALU.mult)
                        ins.then_inc(conv_made, 1)
                    if i >= 13:
                        conv_low(l, i - 13)
                    if q >= 2:
                        stage(pair + 4 + i // 4, q - 2, KD)
                conv_low(l, 3)
                pool_low(l)

                def gate(jj, u, gg, b):
                    hf = (0, 0, 1, 1, 0, 1)[jj]
                    dve.wait_ge(group_done, gg + 1)
                    dve.wait_ge(sig_done, u + jj + 1)
                    take_scaled(scaled[jj % 2][:, :], b, hf).then_inc(evac, 1)

                def merge(hf, gg, r):
                    for b in range(3):
                        dve.wait_ge(group_done, gg + b + 1)
                        if b == 0:
                            dve.wait_ge(sig_done, r[0])
                            if r[2] is not None:
                                dve.wait_ge(*r[2])
                            dve.tensor_tensor(xv[hf][:, :], bank(1), sig[hf][:, :], ALU.mult).then_inc(evac, 1)
                            continue
                        dve.tensor_tensor(tb[b % 2][:, :], bank(1 + b), sig[2 * b + hf][:, :], ALU.mult).then_inc(evac, 1)
                        dve.wait_ge(evac, gg + b + 5)
                        ins = dve.tensor_tensor(xv[hf][:, :], xv[hf][:, :], tb[b % 2][:, :], ALU.add)
                        if b == 1:
                            own_.inc(ins)
                            own_.wait()
                        else:
                            ins.then_inc(merged, 1)

                def merged_low(m, hf):
                    dve.wait_ge(mg_hi_made, 2 * KD * l + 2 * m + hf + 1)
                    dve.tensor_tensor(at_tile(mg_lo, m, hf), xv[hf][:, :], f32(at_tile(mg_hi, m, hf)),
                                      ALU.subtract).then_inc(mg_ready, 1)

                with dve.Fori(0, KD) as m:
                    own_.loop(m, 2)
                    pm, gm, u = pair + MIX_PROJ + 2 * m, g + 4 * MIX_PROJ + 12 * m, 6 * KD * l + 6 * m
                    gate(0, u, gm, 0)
                    gate(1, u, gm + 1, 1)
                    gate(2, u, gm + 2, 2)
                    stage(pm + 1, 0, KD)
                    gate(3, u, gm + 3, 3)
                    stage(pm + 1, 1, KD)
                    gate(4, u, gm + 4, 0)
                    merge(0, gm + 5, (u + 7, None, None))
                    merged_low(m, 0)
                    gate(5, u, gm + 8, 0)
                    stage(pm + 2, 0, KD)
                    merge(1, gm + 9, (u + 8, None, None))
                    stage(pm + 2, 1, KD)
                    merged_low(m, 1)
                    own_.end(KD)
                po, go = pair + MIX_PROJ + 2 * KD, g + 4 * MIX_PROJ + 12 * KD
                with dve.Fori(0, KD // 2 - 2) as i:
                    for q in range(4):
                        take_y(y_mix, i, q, go + 4 * i, False)
                        if q >= 2:
                            stage(po + i + 1, q - 2, KD)
                seam(sm, y_mix, False, po + KD // 2 - 2, go + 2 * KD - 8, KD, "out_last", l, 3, l, 4)

            dve.memset(acc_y[1][:, :], 0.0)
            for q in range(2):
                off = wp[HD * q:HD * q + HD, :].rearrange("p (a q c) -> p a q c", q=2, c=HD)
                dve.memset(off[:, :, 1 - q, :], 0.0)
            dve.memset(eps1[:, :], EPS)
            dve.memset(eps4[:, :], 4 * EPS)
            dve.nop().then_inc(w_split, 2)
            dve.nop().then_inc(evac, 4)
            dve.nop().then_inc(inv_made, 2)
            for d in diag:
                ins = dve.memset(d[:, :], 0.0)
            ins.then_inc(zeroed, 1)
            for k in range(KD):
                dve.wait_ge(x_turned, k + 1)
                dve.tensor_copy(h[:, k * NT:k * NT + 3 * P], ps[:, k, 0:3 * P]).then_inc(h_ready, 1)
            for k in range(KD):
                dve.wait_ge(x_turned, KD + k + 1)
                dve.tensor_copy(h[:, k * NT + 3 * P:(k + 1) * NT], ps[:, k, 0:2 * P]).then_inc(h_ready, 1)
            stage(0, 0, KD)
            stage(0, 1, KD)
            for j in range(8):
                x_low(j, 0, 0, 0)
            dve.wait_ge(ident_in, 16)
            stage(1, 0, KD, "first")
            stage(1, 1, KD, "first")
            inverse(-1, 2)

            with dve.Fori(0, DEPTH) as l:
                own_.loop(l, DVE_STEPS)
                ffn(0, l, 3 * l, l, 2)
                mixer(l, 3 * l + 1)
                ffn(1, l, 3 * l + 2, (l + 1) % DEPTH, 0)
                own_.end(DEPTH)

            dve.wait_ge(out_turned, 4)
            for b in range(3, 5):
                dve.tensor_copy(rows[:, b * D + 512:(b + 1) * D], ps[:, OUT_BANKS[1][b - 2], :]).then_inc(out_dve, 1)

        @block.gpsimd
        def _(pool):
            own_ = Own(pool, pool_step)

            def add_square(acc, q, pos):
                pool.wait_ge(sq_made, q + pos + 1)
                pool.wait_ge(sq_added, q + pos + 2)
                pool.tensor_tensor(acc[:, :], acc[:, :], sq[pos % 2][:, :], ALU.add).then_inc(sq_added, 1)

            def clear(acc, s_index):
                pool.wait_ge(sum_done, s_index + 1)
                alone(pool)
                own_.inc(pool.memset(acc[:, :], 0.0))

            def seam(n, order):
                q = SQUARES * (n + 1)
                for i, (what, j) in enumerate(order):
                    add_square(acc_y[j // KD] if what == "y" else acc_x[0], q, 8 + i)

            def begin(n):
                for j in range(8, 16):
                    add_square(acc_x[1], SQUARES * (n + 1), 16 + j)
                clear(acc_y[0], 4 * (n + 1))
                clear(acc_y[1], 4 * (n + 1) + 1)
                clear(acc_x[0], 4 * (n + 1) + 2)
                clear(acc_x[1], 4 * (n + 1) + 3)
                own_.wait()
                alone(pool)

            def ffn(n, l, sm):
                begin(sm - 1)
                for fg in range(2):
                    unit = l * 8 * FG + n * 4 * FG + fg * 2 * FG
                    if fg == 0:
                        for u in range(4):
                            pool.wait_ge(mid_hi_made, unit + u + 1)
                            pool.tensor_tensor(tile(mid_lo, u % 2, u // 2), mid[u % 2][:, :], f32(tile(mid_hi, u % 2, u // 2)),
                                               ALU.subtract).then_inc(mid_split, 1)
                    with pool.Fori(2 - 2 * fg, FG) as f:
                        for hf in range(2):
                            pool.wait_ge(mid_hi_made, unit + 2 * f + hf + 1)
                            pool.tensor_tensor(at_tile(mid_lo, f, hf), mid[hf][:, :], f32(at_tile(mid_hi, f, hf)),
                                               ALU.subtract).then_inc(mid_split, 1)
                with pool.Fori(0, KD // 2 - 2) as i:
                    for q in range(4):
                        add_square(acc_y[q // 2], SQUARES * (sm + 1) + 4 * i, q)
                seam(sm, SEAM_SQ)

            def mixer(l, sm):
                g = l * GROUPS + MIX_GROUP0
                begin(sm - 1)
                pool.wait_ge(const_in, 16 * CONST_DMAS)
                own_.inc(pool.tensor_copy(wc_now[:, :], prm[:, ds(l * NPC + PC_WC, 6)]))
                for t in range(2):
                    pool.memset(p_ext[:, t * PE_W:t * PE_W + PH], 0.0)
                    own_.inc(pool.memset(c_ext[:, t * CE_W:t * CE_W + CH_], 0.0))
                own_.wait()
                pool.wait_ge(turned_out, 4 * l + 1)
                pool.wait_ge(evac, g + 12 + 8)

                def window(dst, src, back, lo, hi):
                    a = 2 * back - 1
                    own_.inc(pool.tensor_tensor(dst[lo:hi, a:PE_W], src[lo:hi, a:PE_W],
                                                src[lo:hi, a - back:PE_W - back], ALU.add))
                    own_.wait()

                for t in range(2):
                    src = p_ext[:, t * PE_W:(t + 1) * PE_W]
                    if t == 0:
                        window(win_v, src, 1, 0, HD)
                        window(win_a, src, 1, HD, P)
                        window(win_v, win_a, 2, HD, P)
                    else:
                        window(win_a, src, 1, 0, P)
                        window(win_b, win_a, 2, 0, P)
                        window(win_v, win_b, 4, 0, HD)
                        window(win_a, win_b, 4, HD, P)
                        window(win_v, win_a, 8, HD, P)
                    cnt = count[:, t * 17:t * 17 + 17]
                    smp = [b_[:, PH + SEQ:PE_W].rearrange("p (b t) -> p b t", b=DEC_B)[:, :, PH:] for b_ in (win_v, src)]
                    dp = tile(d_pool, t)
                    d_smp = dp[:, SEQ:NT].rearrange("p (b t) -> p b t", b=DEC_B)
                    pool.tensor_tensor(dp[:, 0:16], win_v[:, PH:PH + 16], cnt[:, 0:16], ALU.mult)
                    pool.tensor_scalar(dp[:, 16:SEQ], win_v[:, PH + 16:PH + SEQ], cnt[:, 16:17], 1.0, ALU.mult, ALU.mult)
                    own_.inc(pool.tensor_scalar(d_smp, smp[0], cnt[:, 16:17], 1.0, ALU.mult, ALU.mult))
                    own_.wait()
                    pool.tensor_tensor(dp[:, 0:SEQ], dp[:, 0:SEQ], src[:, PH:PH + SEQ], ALU.subtract)
                    ins = pool.tensor_tensor(d_smp, d_smp, smp[1], ALU.subtract)
                    if t == 1:
                        ins.then_inc(d_made, 1)
                n = CE_W - 2
                for t in range(2):
                    z, term = (win_a, win_b)[t][:, 0:n], win_v[:, 0:n]
                    src = c_ext[:, t * CE_W:(t + 1) * CE_W]

                    def times(dst, j):
                        return pool.tensor_scalar(dst, src[:, j:n + j], wc_now[:, 2 * j + t:2 * j + t + 1], 1.0, ALU.mult, ALU.mult)

                    if t == 1:
                        pool.wait_ge(z_made, 2 * l + 1)
                    pool.wait_ge(evac, g + 16 + 4 * t + 8)
                    alone(pool)
                    times(z, 0)
                    own_.inc(times(term, 1))
                    own_.wait()
                    own_.inc(pool.tensor_tensor(z, z, term, ALU.add))
                    own_.wait()
                    alone(pool)
                    own_.inc(times(term, 2))
                    own_.wait()
                    pool.tensor_tensor(z, z, term, ALU.add).then_inc(z_made, 1)
                with pool.Fori(0, KD // 2 - 2) as i:
                    for q in range(4):
                        add_square(acc_y[q // 2], SQUARES * (sm + 1) + 4 * i, q)
                seam(sm, SEAM_SQ_MIX)

            for a in (acc_x[0], acc_x[1], acc_y[0]):
                own_.inc(pool.memset(a[:, :], 0.0))
            pool.nop().then_inc(mid_split, 2)
            pool.nop().then_inc(sq_added, 18)
            own_.wait()
            for j in range(KD):
                add_square(acc_x[0], 0, 16 + j)
            with pool.Fori(0, DEPTH) as l:
                own_.loop(l, POOL_STEPS)
                ffn(0, l, 3 * l)
                mixer(l, 3 * l + 1)
                ffn(1, l, 3 * l + 2)
                own_.end(DEPTH)


_INS = ["x_prompt", "x_sample", "state_pool", "state_conv", "cache_k", "cache_v", "norm_g", "ffn1_w_gate",
        "ffn1_w_up", "ffn1_w_down", "w_in", "b_gate", "w_pool", "pool_scale", "sinks", "w_conv", "w_branch",
        "w_out", "ffn2_w_gate", "ffn2_w_up", "ffn2_w_down"]
_OUTS = [(1, SEQ, D), (DEC_B, DEC_T, D), (DEPTH, 1, PH, PW), (DEPTH, 1, CH_, CW), (DEPTH, 1, WIN, NKV, HD),
         (DEPTH, 1, WIN, NKV, HD), (DEPTH, DEC_B, PH, PW), (DEPTH, DEC_B, CH_, CW), (DEPTH, DEC_B, WIN, NKV, HD),
         (DEPTH, DEC_B, WIN, NKV, HD)]


def constants():
    windows = (2, 4, 8, 16)
    cnt = np.zeros((P, 2, 17), np.float32)
    for t in range(2):
        for p in range(P):
            w = windows[2 * t + p // HD]
            cnt[p, t, :16] = 1.0 / np.minimum(np.arange(16) + 1, w)
            cnt[p, t, 16] = 1.0 / w
    return {"c_ident": np.eye(P, dtype=np.float32), "c_ones": np.ones((P, P), np.float32),
            "c_count": cnt.reshape(P, 34)}


def kernel(**inputs):
    import concourse.bacc as _bacc
    from concourse.bass_utils import run_bass_kernel_spmd as _run

    nc = _bacc.Bacc("TRN2", target_bir_lowering=False, num_devices=1, dynamic_dma_scratch_size=1024)
    arrays, args = {}, []
    given = {name: np.ascontiguousarray(inputs[name]) for name in _INS} | constants()
    for name, a in given.items():
        arrays[f"in_{name}_dram"] = a
        args.append(nc.dram_tensor(f"in_{name}_dram", a.shape, F32, kind="ExternalInput").ap())
    for i, shape in enumerate(_OUTS):
        args.append(nc.dram_tensor(f"out_{i}_dram", shape, F32, kind="ExternalOutput").ap())
    trunk_kernel(nc, *args)
    r = _run(nc, [arrays], core_ids=[0])
    return tuple(r.results[0][f"out_{i}_dram"] for i in range(len(_OUTS)))
```
